# Optimizing a Trainium2 kernel written in Bass

```python
import jax, jax.numpy as jnp
from jax import lax
import numpy as np

D_MODEL = 1024
BATCH = 1
SEQ = 1024
DEPTH = 2

D_MIX = D_MODEL
POOL_WIDTH = D_MIX // 2
POOL_WINDOWS = (2, 4, 8, 16)
POOL_GROUPS = len(POOL_WINDOWS)
POOL_GROUP_DIM = POOL_WIDTH // POOL_GROUPS
SGU_WIDTH = D_MIX - POOL_WIDTH
SGU_HEADS = 4
SGU_HEAD_DIM = SGU_WIDTH // SGU_HEADS
CHUNK = 128
EVEN_IN = POOL_WIDTH + 2 * SGU_WIDTH
CONV_WIDTH = 3
CONV_DIM = D_MIX
D_FF = 4 * D_MODEL
PLE_DIM = 256
LN_EPS = 1e-5
N_EVEN = (DEPTH + 1) // 2
N_ODD = DEPTH // 2
DEEPNORM_ALPHA = (2.0 * DEPTH) ** 0.25
DEEPNORM_BETA = (8.0 * DEPTH) ** -0.25

kernel_name = "hybrid_pool_sgu_shortconv_deepnorm_trunk"

def layer_norm(x, g, b):
    xf = x.astype(jnp.float32)
    mu = jnp.mean(xf, axis=-1, keepdims=True)
    var = jnp.mean(jnp.square(xf - mu), axis=-1, keepdims=True)
    y = (xf - mu) * lax.rsqrt(var + LN_EPS)
    return (y * g.astype(jnp.float32) + b.astype(jnp.float32)).astype(x.dtype)

def pool_mixer(a, pool_w, pool_scale):
    bsz, s, _ = a.shape
    ag = a.reshape(bsz, s, POOL_GROUPS, POOL_GROUP_DIM)
    t = jnp.arange(s)
    outs = []
    for g, w in enumerate(POOL_WINDOWS):
        xg = ag[:, :, g].astype(jnp.float32)
        cs = jnp.cumsum(xg, axis=1)
        lag = jnp.pad(cs, ((0, 0), (w, 0), (0, 0)))[:, :s]
        cnt = jnp.minimum(t + 1, w).astype(jnp.float32)[None, :, None]
        pooled = (cs - lag) / cnt - xg
        outs.append(jnp.einsum('bsc,cd->bsd', pooled.astype(a.dtype), pool_w[g]))
    return jnp.concatenate(outs, axis=-1) * pool_scale

def spatial_gating(u, v, ln_g, ln_b, w_s, b_s):
    bsz, s, _ = u.shape
    vn = layer_norm(v, ln_g, ln_b)
    vc = vn.reshape(bsz, s // CHUNK, CHUNK, SGU_HEADS, SGU_HEAD_DIM)
    mask = jnp.tril(jnp.ones((CHUNK, CHUNK), w_s.dtype))
    mixed = jnp.einsum('hts,bnshc->bnthc', w_s * mask, vc) + b_s.T[None, None, :, :, None]
    return u * mixed.reshape(bsz, s, SGU_WIDTH)

def short_conv_mixer(x, w_in, conv_w, w_out):
    proj = jnp.einsum('bsd,de->bse', x, w_in)
    gate_b, gate_c, h = jnp.split(proj, 3, axis=-1)
    z = gate_c * h
    zp = jnp.pad(z, ((0, 0), (CONV_WIDTH - 1, 0), (0, 0)))
    s = x.shape[1]
    conv = sum(conv_w[k] * zp[:, k:k + s] for k in range(CONV_WIDTH))
    return jnp.einsum('bse,ed->bsd', gate_b * conv, w_out)

def setup_inputs(seed: int = 0) -> dict:
    key = jax.random.key(seed)
    ks = jax.random.split(key, 24)
    f32 = jnp.float32
    nrm = lambda k, shape, scale: jax.random.normal(k, shape, f32) * scale
    return {
        "x": nrm(ks[0], (BATCH, SEQ, D_MODEL), 1.0),
        "p": nrm(ks[1], (DEPTH, BATCH, SEQ, PLE_DIM), 1.0),
        "ev_w_in": nrm(ks[2], (N_EVEN, D_MODEL, EVEN_IN), D_MODEL ** -0.5),
        "ev_pool_w": nrm(ks[3], (N_EVEN, POOL_GROUPS, POOL_GROUP_DIM, POOL_GROUP_DIM), POOL_GROUP_DIM ** -0.5),
        "ev_pool_scale": 1.0 + nrm(ks[4], (N_EVEN, POOL_WIDTH), 0.05),
        "ev_sgu_ln_g": 1.0 + nrm(ks[5], (N_EVEN, SGU_WIDTH), 0.05),
        "ev_sgu_ln_b": nrm(ks[6], (N_EVEN, SGU_WIDTH), 0.02),
        "ev_sgu_w": nrm(ks[7], (N_EVEN, SGU_HEADS, CHUNK, CHUNK), CHUNK ** -0.5),
        "ev_sgu_b": 1.0 + nrm(ks[8], (N_EVEN, SGU_HEADS, CHUNK), 0.01),
        "ev_w_out": nrm(ks[9], (N_EVEN, D_MIX, D_MODEL), D_MIX ** -0.5 * DEEPNORM_BETA),
        "od_w_in": nrm(ks[10], (N_ODD, D_MODEL, 3 * CONV_DIM), D_MODEL ** -0.5),
        "od_conv_w": nrm(ks[11], (N_ODD, CONV_WIDTH, CONV_DIM), CONV_WIDTH ** -0.5),
        "od_w_out": nrm(ks[12], (N_ODD, CONV_DIM, D_MODEL), CONV_DIM ** -0.5 * DEEPNORM_BETA),
        "ln1_g": 1.0 + nrm(ks[13], (DEPTH, D_MODEL), 0.05),
        "ln1_b": nrm(ks[14], (DEPTH, D_MODEL), 0.02),
        "ffn_w1": nrm(ks[15], (DEPTH, D_MODEL, D_FF), D_MODEL ** -0.5),
        "ffn_w2": nrm(ks[16], (DEPTH, D_FF, D_MODEL), D_FF ** -0.5 * DEEPNORM_BETA),
        "ln2_g": 1.0 + nrm(ks[17], (DEPTH, D_MODEL), 0.05),
        "ln2_b": nrm(ks[18], (DEPTH, D_MODEL), 0.02),
        "ple_gate_w": nrm(ks[19], (DEPTH, D_MODEL, D_MODEL), D_MODEL ** -0.5),
        "ple_w": nrm(ks[20], (DEPTH, PLE_DIM, D_MODEL), PLE_DIM ** -0.5),
    }

def reference(x, p, ev_w_in, ev_pool_w, ev_pool_scale, ev_sgu_ln_g, ev_sgu_ln_b,
              ev_sgu_w, ev_sgu_b, ev_w_out, od_w_in, od_conv_w, od_w_out,
              ln1_g, ln1_b, ffn_w1, ffn_w2, ln2_g, ln2_b, ple_gate_w, ple_w):
    for i in range(DEPTH):
        j = i // 2
        if i % 2 == 0:
            proj = jnp.einsum('bsd,de->bse', x, ev_w_in[j])
            a = proj[..., :POOL_WIDTH]
            u = proj[..., POOL_WIDTH:POOL_WIDTH + SGU_WIDTH]
            v = proj[..., POOL_WIDTH + SGU_WIDTH:]
            y_a = pool_mixer(a, ev_pool_w[j], ev_pool_scale[j])
            y_b = spatial_gating(u, v, ev_sgu_ln_g[j], ev_sgu_ln_b[j], ev_sgu_w[j], ev_sgu_b[j])
            mix = jnp.einsum('bse,ed->bsd', jnp.concatenate([y_a, y_b], axis=-1), ev_w_out[j])
        else:
            mix = short_conv_mixer(x, od_w_in[j], od_conv_w[j], od_w_out[j])
        x = layer_norm(DEEPNORM_ALPHA * x + mix, ln1_g[i], ln1_b[i])
        hid = jnp.square(jax.nn.relu(jnp.einsum('bsd,df->bsf', x, ffn_w1[i])))
        x = layer_norm(DEEPNORM_ALPHA * x + jnp.einsum('bsf,fd->bsd', hid, ffn_w2[i]), ln2_g[i], ln2_b[i])
        gate = jax.nn.sigmoid(jnp.einsum('bsd,de->bse', x, ple_gate_w[i]))
        x = x + gate * jnp.einsum('bsk,kd->bsd', p[i], ple_w[i])
    return x


_drawn_inputs = setup_inputs


def setup_inputs(seed=0):
    import zlib

    import numpy as np

    out = dict(_drawn_inputs(seed))
    spreads = {}
    factors = {'ev_pool_scale': 5.733, 'ev_sgu_ln_g': 6.822, 'ev_sgu_ln_b': 8.0, 'ev_sgu_b': 8.0}
    for name, (base, spread) in spreads.items():
        noise = np.random.default_rng([zlib.crc32(name.encode()), seed]).standard_normal(out[name].shape)
        drawn = base * np.exp(spread * noise) if base else spread * noise
        out[name] = __import__('jax').numpy.asarray(drawn.astype(out[name].dtype))
    for name, factor in factors.items():
        out[name] = (out[name] * factor).astype(out[name].dtype)
    return out
```

```python
from contextlib import ExitStack

import concourse.bass as bass
from concourse import mybir

P = 128
F32 = mybir.dt.float32
F32R = mybir.dt.float32r
ALU = mybir.AluOpType
ACT = mybir.ActivationFunctionType

SEQ = 1024
D = 1024
KT = D // P
TT = SEQ // P
HALF = 512
HT = HALF // P
BLK = 256
BT = BLK // P
WIDTH = 512
FF = 4 * D
FFN_BLOCKS = FF // BLK
OD_BLOCKS = D // BLK
PLE = 256
PIECE = 512
NRAW = 4
NTMP = 4
RING = 4
WINDOWS = (2, 4, 8, 16)
PAD = 16
EPS = 1e-5
ALPHA = 4.0 ** 0.25

ROW_G = (0, 32)
ROW_B = (16, 48)
ROW_POOL = 64
ROW_CONV = 68
ROWS = 92


class Stage:

    def __init__(self, kind, at, half=0, blk=0, g=0, js=(), tiles=(), source=None, layer=0, ln=None, col=0,
                 first=False, cur=0, body=(), trips=0):
        self.kind = kind
        self.at = dict(at)
        self.i = 0
        self.step = {}
        self.half, self.blk, self.g, self.js, self.tiles = half, blk, g, js, tiles
        self.source, self.layer, self.ln, self.col = source, layer, ln, col
        self.first, self.cur = first, cur
        self.body, self.trips = body, trips
        self.need_x, self.need_h = [0, 0], [0, 0]
        self.ga, self.gb, self.unit = at["ga"], at["gb"], at["unit"]
        self.moved, self.mixg, self.conv, self.dval = at["moved"], at["mixg"], at["conv"], at["dval"]
        self.xnew, self.accd, self.piece = at["xnew"], at["accd"], at["piece"]

    def n(self, name, k=0):
        v = self.at[name] + k
        return v + self.i * self.step[name] if name in self.step else v

    def later(self, value, name):
        return value + self.i * self.step[name] if name in self.step else value


COUNTS = ("ga", "gb", "unit", "aval", "dval", "moved", "conv", "xnew", "accd", "slab", "piece")
ADDS = {
    "consts": dict(ga=2, moved=2),
    "turn_p": dict(ga=2, unit=2, aval=2),
    "u": dict(ga=2, moved=2),
    "mix": dict(ga=2, unit=2, dval=2),
    "a": dict(ga=1, moved=1),
    "lin": dict(ga=2, unit=2, aval=2),
    "c": dict(ga=2, moved=2),
    "h": dict(ga=2, conv=2),
    "bgate": dict(ga=2, unit=2, dval=2),
    "ffn": dict(ga=2, unit=2, aval=2, dval=2),
    "alpha": dict(accd=HT),
    "affine": dict(accd=HT),
    "vln": {}, "stats": {},
}
FREED_BY = dict(consts="moved", turn="aval", turn_p="aval", u="moved", mix="mixg", a="moved", lin="aval", c="moved",
                h="conv", bgate="dval", ffn="aval")


def make_plan():
    at = dict.fromkeys(COUNTS, 0)
    at["mixg"] = 0
    plan, freed, slab_end, slabs = [], [], [], []
    need = dict(xu=[0, 0], hu=[0, 0])
    where = [plan]

    def add(kind, slab=None, last=False, **args):
        if slab is not None:
            slabs.append((slab, at["piece"]))
            at["slab"] += 1
            at["piece"] += 5 if slab[0] == "gate" else 4
        st = Stage(kind, at, first=slab is not None, cur=at["slab"] - 1, **args)
        st.need_x, st.need_h = list(need["xu"]), list(need["hu"])
        adds = dict(ADDS.get(kind, {}))
        if kind in ("out", "gate", "v"):
            adds["gb"] = len(args["tiles"]) * (2 if kind == "out" else 1)
            if kind == "gate":
                adds["xnew"] = len(args["tiles"])
        if kind == "turn":
            adds.update(ga=len(args["js"]), unit=len(args["js"]), aval=len(args["js"]))
        if kind == "mix":
            adds["mixg"] = 2
        by = FREED_BY.get(kind)
        for k in range(adds.get("ga", 0)):
            freed.append((by, at[by] + k + 1))
        for name, k in adds.items():
            at[name] += k
        if kind == "turn":
            need["xu"][st.half] = at["unit"]
        if kind in ("turn_p", "mix", "lin", "bgate", "ffn"):
            need["hu"][st.half] = at["unit"]
        if last:
            slab_end.append(("ga", at["ga"]) if kind in ("u", "a", "c", "h", "bgate", "ffn") else ("gb", at["gb"]))
        where[-1].append(st)
        return st

    lo, hi = list(range(HT)), list(range(HT, TT))

    def turns(source, half, js, layer=0, n=0):
        add("turn", source=source, half=half, js=js, layer=layer, ln=n)

    def block_out(rows, ln=None, layer=0, p=False):
        add("out", slab=rows, tiles=lo)
        if ln is None:
            add("out", tiles=hi, last=True)
            return
        add("stats", half=0, ln=ln)
        add("out", tiles=[4, 5])
        turns("ln", 0, [0, 1, 2, 3], n=ln)
        add("out", tiles=[6])
        turns("ln", 0, [4, 5, 6, 7], n=ln)
        if p:
            add("turn_p", half=0, layer=layer)
        add("out", tiles=[7], last=True)
        add("stats", half=1, ln=ln)
        add("affine", half=0, ln=ln)

    def second_half(ln=None, p=False, layer=0):
        turns("ln", 1, list(range(KT)), n=ln)
        if p:
            add("turn_p", half=1, layer=layer)
        add("affine", half=1, ln=ln)

    def ffn(layer):
        add("ffn", slab=("w1", layer, 0), half=0)
        second_half(ln=2 * layer)
        add("ffn", half=1, last=True)
        block_out(("w2", layer, 0))
        body, before = [], dict(at)
        where.append(body)
        add("ffn", slab=("w1", layer, "loop"), half=0)
        add("ffn", half=1, last=True)
        block_out(("w2", layer, "loop"))
        where.pop()
        trips = FFN_BLOCKS - 2
        step = {k: at[k] - before[k] for k in at if at[k] != before[k]}
        for st in body:
            st.step = step
        loop = Stage("loop", before, body=body, trips=trips, layer=layer)
        where[-1].append(loop)
        for k, v in step.items():
            at[k] += v * (trips - 1)
        need["hu"] = [x + step["unit"] * (trips - 1) for x in need["hu"]]
        la, ls = step["ga"], step["slab"]
        for t in range(1, trips):
            for name, v in freed[-la:]:
                freed.append((name, v + step[name]))
            for name, v in slab_end[-ls:]:
                slab_end.append((name, v + step[name]))
        for t in range(1, trips):
            slabs.extend([None] * ls)
        add("ffn", slab=("w1", layer, FFN_BLOCKS - 1), half=0)
        add("ffn", half=1, last=True)
        block_out(("w2", layer, FFN_BLOCKS - 1), ln=2 * layer + 1, layer=layer, p=True)

    def gates(layer):
        for c in range(4):
            add("gate", slab=("gate", layer, c), tiles=lo, col=c, layer=layer)
            if c == 0:
                second_half(ln=2 * layer + 1, p=True, layer=layer)
            if c < 3 or layer == 1:
                add("gate", tiles=hi, col=c, layer=layer, last=True)
                continue
            add("gate", tiles=[4, 5], col=c, layer=layer)
            turns("gate", 0, [0, 1, 2, 3])
            add("gate", tiles=[6], col=c, layer=layer)
            turns("gate", 0, [4, 5, 6, 7])
            add("gate", tiles=[7], col=c, layer=layer, last=True)

    add("consts")
    turns("input", 0, list(range(KT)))
    add("v", slab=("ev", 4 * BLK), tiles=lo, col=0)
    turns("input", 1, list(range(KT)))
    add("alpha", half=0)
    add("alpha", half=1)
    add("v", tiles=hi, col=0, last=True)
    add("v", slab=("ev", 5 * BLK), tiles=lo, col=1)
    add("vln", half=0)
    add("v", tiles=hi, col=1, last=True)
    add("vln", half=1)
    for blk in range(2):
        add("u", slab=("ev", WIDTH + blk * BLK), half=0, blk=blk)
        add("mix", half=0, blk=blk)
        add("u", half=1, blk=blk, last=True)
        add("mix", half=1, blk=blk)
        block_out(("ev_out", WIDTH + blk * BLK))
    for blk in range(2):
        add("a", slab=("ev", blk * BLK), half=0, blk=blk, g=0)
        add("a", half=0, blk=blk, g=1)
        add("a", half=1, blk=blk, g=0)
        add("lin", half=0, blk=blk)
        add("a", half=1, blk=blk, g=1, last=True)
        rows = ("ev_out", blk * BLK)
        add("out", slab=rows, tiles=[0, 1, 2])
        add("lin", half=1, blk=blk)
        add("out", tiles=[3])
        if blk == 0:
            add("out", tiles=hi, last=True)
    add("stats", half=0, ln=0)
    add("out", tiles=[4, 5])
    turns("ln", 0, [0, 1, 2, 3], n=0)
    add("out", tiles=[6])
    turns("ln", 0, [4, 5, 6, 7], n=0)
    add("out", tiles=[7], last=True)
    add("stats", half=1, ln=0)
    add("affine", half=0, ln=0)
    ffn(0)
    gates(0)
    for blk in range(OD_BLOCKS):
        add("c", slab=("od", D + blk * BLK), half=0, blk=blk)
        if blk == 0:
            turns("gate", 1, list(range(KT)))
            add("alpha", half=0)
            add("alpha", half=1)
        add("c", half=1, blk=blk, last=True)
        add("h", slab=("od", 2 * D + blk * BLK), half=0, blk=blk)
        add("h", half=1, blk=blk, last=True)
        add("bgate", slab=("od", blk * BLK), half=0, blk=blk)
        add("bgate", half=1, blk=blk, last=True)
        block_out(("od_out", blk * BLK), ln=2 if blk == OD_BLOCKS - 1 else None)
    ffn(1)
    gates(1)
    return plan, freed, slab_end, slabs, dict(at)


def trunk(nc, x, p, ev_w_in, ev_pool_w, ev_pool_scale, ev_sgu_ln_g, ev_sgu_ln_b, ev_sgu_w, ev_sgu_b, ev_w_out,
          od_w_in, od_conv_w, od_w_out, ln1_g, ln1_b, ffn_w1, ffn_w2, ln2_g, ln2_b, ple_gate_w, ple_w, out):
    plan, freed, slab_end, slabs, total = make_plan()
    n_slabs = total["slab"]

    x_v = x[0].rearrange("(t p) d -> p t d", p=P)
    out_v = out[0].rearrange("(t p) d -> p t d", p=P)

    with ExitStack() as ctx:
        def sb(name, shape, dt=F32):
            return ctx.enter_context(nc.sbuf_tensor(name, shape, dt))

        def sem(name):
            return ctx.enter_context(nc.semaphore(name))

        resid = sb("resid", [P, TT, D])
        xt_hi = sb("xt_hi", [P, KT, SEQ], F32R)
        xt_lo = sb("xt_lo", [P, KT, SEQ], F32R)
        hid_hi = sb("hid_hi", [P, BT, SEQ], F32R)
        hid_lo = sb("hid_lo", [P, BT, SEQ], F32R)
        w_hi = sb("w_hi", [P, 2, 5 * PIECE], F32R)
        w_lo = sb("w_lo", [P, 2, 5 * PIECE], F32R)
        raw = sb("raw", [P, NRAW, PIECE])
        tmp = sb("tmp", [P, NTMP, HALF])
        gb_rows = sb("gb_rows", [P, 2, D])
        scratch = sb("scratch", [P, 6144])
        shared = sb("shared", [P, 512])
        ident = sb("ident", [P, P])
        ws_t = sb("ws_t", [P, 4, P])
        cols = sb("cols", [P, ROWS])
        inv_cnt = sb("inv_cnt", [P, PAD])
        bn6 = sb("bn6", [P, HT, 12])
        mean_var = sb("mean_var", [P, HT, 2])
        var_eps = sb("var_eps", [P, HT])
        std = sb("std", [P, HT])
        rstd = sb("rstd", [P, HT])
        newton = sb("newton", [P, HT])
        neg_mean = sb("neg_mean", [P, HT])

        v_n = scratch[:, 0:4096].rearrange("p (t c) -> p t c", t=TT)
        u_t = scratch[:, 4096:6144].rearrange("p (g s) -> p g s", g=BT)
        a_t = scratch[:, 0:2 * (PAD + SEQ)].rearrange("p (g s) -> p g s", g=BT)
        win0 = 2 * (PAD + SEQ)
        win = scratch[:, win0:win0 + 2 * (PAD + HALF)].rearrange("p (b s) -> p b s", b=2)
        pooled0 = win0 + 2 * (PAD + HALF)
        pooled = scratch[:, pooled0:pooled0 + 2 * SEQ].rearrange("p (g s) -> p g s", g=BT)
        cv = scratch[:, 0:2 * SEQ].rearrange("p (g s) -> p g s", g=BT)
        z = scratch[:, 2 * SEQ:2 * SEQ + 2 * (SEQ + 2)].rearrange("p (g s) -> p g s", g=BT)
        p_n = scratch[:, 0:TT * PLE].rearrange("p (t k) -> p t k", t=TT)
        ws_n = scratch[:, 4096:4608].rearrange("p (h s) -> p h s", h=4)
        rows_n = scratch[0:ROWS, 4608:4736]
        pool_w = shared[:, :].rearrange("p (g d) -> p g d", g=4)
        sig = shared[:, :].rearrange("p (b c) -> p b c", b=2)
        sgu_b = gb_rows[:, 0, 512:1024].rearrange("p (h t) -> p h t", h=4)

        bank_a = [ctx.enter_context(nc.psum_tensor(f"bank_a{k}", [P, HALF], F32)) for k in range(RING)]
        bank_b = [ctx.enter_context(nc.psum_tensor(f"bank_b{k}", [P, HALF], F32)) for k in range(RING)]

        x_in = [sem("x_in0"), sem("x_in1")]
        param_in = sem("param_in")
        late_in = sem("late_in")
        gb_in = sem("gb_in")
        p_in = sem("p_in")
        raw_in = [sem(f"raw_in{k}") for k in range(NRAW)]
        hi_split = sem("hi_split")
        lo_split = sem("lo_split")
        a_full = sem("a_full")
        b_full = sem("b_full")
        b_free = sem("b_free")
        act_value = sem("act_value")
        dve_value = sem("dve_value")
        moved = sem("moved")
        mix_read = sem("mix_read")
        z_ready = sem("z_ready")
        conv_step = sem("conv_step")
        window_step = sem("window_step")
        unit_hi = sem("unit_hi")
        unit_lo = sem("unit_lo")
        var_ready = sem("var_ready")
        std_ready = sem("std_ready")
        norm_ready = sem("norm_ready")
        xn_act = sem("xn_act")
        xn_dve = sem("xn_dve")
        vn_ready = sem("vn_ready")
        gained = sem("gained")
        gb_scaled = sem("gb_scaled")
        acc_ready = sem("acc_ready")
        sig_ready = sem("sig_ready")
        x_new = sem("x_new")
        ln_step = sem("ln_step")
        ident_step = sem("ident_step")
        dve_const = sem("dve_const")
        out_done = sem("out_done")

        sem_of = dict(aval=act_value, moved=moved, mixg=mix_read, conv=z_ready, dval=dve_value, ga=a_full, gb=b_full)

        def walk(visit, loop):
            for st in plan:
                if st.kind != "loop":
                    visit(st)
                    continue
                with loop(0, st.trips) as i:
                    for part in st.body:
                        part.i = i
                        visit(part)

        block = ctx.enter_context(nc.Block())

        @block.sync
        def _(sp):
            def column_slab(w, col0):
                v = w.rearrange("(q k p) n -> q p k n", k=2, p=P)
                return [v[q, :, :, bass.ds(col0, BLK)] for q in range(4)]

            def row_slab(w, row0):
                return [w[bass.ds(row0 + (q // 2) * P, P), (q % 2) * PIECE:(q % 2 + 1) * PIECE] for q in range(4)]

            def sources(what, i):
                kind = what[0]
                if kind == "ev":
                    return column_slab(ev_w_in[0], what[1])
                if kind == "od":
                    return column_slab(od_w_in[0], what[1])
                if kind == "w1":
                    return column_slab(ffn_w1[what[1]], (i + 1 if what[2] == "loop" else what[2]) * BLK)
                if kind == "w2":
                    return row_slab(ffn_w2[what[1]], (i + 1 if what[2] == "loop" else what[2]) * BLK)
                if kind == "ev_out":
                    return row_slab(ev_w_out[0], what[1])
                if kind == "od_out":
                    return row_slab(od_w_out[0], what[1])
                ple = ple_w[what[1]].rearrange("(k p) n -> p k n", p=P)
                return column_slab(ple_gate_w[what[1]], what[2] * BLK) + [ple[:, :, bass.ds(what[2] * BLK, BLK)]]

            def load_slab(what, piece, i=0):
                for q, src in enumerate(sources(what, i)):
                    n = piece + q
                    if n >= NRAW:
                        sp.wait_ge(lo_split, n - NRAW + 1 + i * 8)
                    dst = raw[:, n % NRAW, :]
                    if len(src.shape) == 3:
                        dst = dst.rearrange("p (k n) -> p k n", k=2)
                    sp.dma_start(dst, src).then_inc(raw_in[n % NRAW], 16)

            def load_gb(gain, bias, width):
                sp.dma_start(gb_rows[:, 0, 0:width], gain.partition_broadcast(P)).then_inc(gb_in, 16)
                sp.dma_start(gb_rows[:, 1, 0:width], bias.partition_broadcast(P)).then_inc(gb_in, 16)

            sp.dma_start(rows_n[0:16, :], ln1_g.rearrange("l (j p) -> (l j) p", p=P)).then_inc(param_in, 16)
            sp.dma_start(rows_n[16:32, :], ln1_b.rearrange("l (j p) -> (l j) p", p=P)).then_inc(param_in, 16)
            sp.dma_start(rows_n[32:48, :], ln2_g.rearrange("l (j p) -> (l j) p", p=P)).then_inc(param_in, 16)
            sp.dma_start(rows_n[48:64, :], ln2_b.rearrange("l (j p) -> (l j) p", p=P)).then_inc(param_in, 16)
            sp.dma_start(rows_n[64:68, :], ev_pool_scale[0].rearrange("(j p) -> j p", p=P)).then_inc(param_in, 16)
            sp.dma_start(rows_n[68:92, :], od_conv_w[0].rearrange("k (j p) -> (k j) p", p=P)).then_inc(param_in, 16)
            sp.dma_start(ws_n, ev_sgu_w[0].rearrange("h t s -> t h s")).then_inc(param_in, 16)
            for t in range(HT):
                sp.dma_start(resid[:, t, :], x_v[:, t, :]).then_inc(x_in[0], 16)
            load_slab(*slabs[0])
            for t in range(HT, TT):
                sp.dma_start(resid[:, t, :], x_v[:, t, :]).then_inc(x_in[1], 16)
            load_gb(ev_sgu_ln_g[0], ev_sgu_ln_b[0], WIDTH)
            sp.dma_start(sgu_b, ev_sgu_b[0].partition_broadcast(P)).then_inc(late_in, 16)
            sp.dma_start(pool_w, ev_pool_w[0].rearrange("g c d -> c g d")).then_inc(late_in, 16)

            def stage(st):
                if st.first and st.cur + 1 < n_slabs and not st.step and slabs[st.cur + 1] is not None:
                    load_slab(*slabs[st.cur + 1])
                if st.kind == "a" and st.first and st.blk == 0:
                    sp.wait_ge(unit_lo, st.unit)
                    load_gb(ln1_g[0], ln1_b[0], D)
                if st.kind == "c" and st.first and st.blk == 1:
                    sp.wait_ge(acc_ready, st.accd - 2 * HT)
                    load_gb(ln1_g[1], ln1_b[1], D)
                if st.kind == "gate" and st.layer == 1 and st.col == 3:
                    for k, t in enumerate(st.tiles):
                        sp.wait_ge(x_new, st.xnew + k + 1)
                        sp.dma_start(out_v[:, t, :], resid[:, t, :]).then_inc(out_done, 16)

            for st in plan:
                if st.kind != "loop":
                    stage(st)
                    continue
                layer = st.layer
                sp.wait_ge(acc_ready, st.accd)
                load_gb(ln2_g[layer], ln2_b[layer], D)
                sp.wait_ge(unit_lo, st.unit)
                sp.dma_start(p_n, p[layer, 0].rearrange("(t q) k -> q t k", q=P)).then_inc(p_in, 16)
                first = slabs[st.body[0].cur]
                second = slabs[st.body[2].cur]
                with sp.Fori(0, st.trips) as i:
                    load_slab(second[0], second[1], i)
                    for q, src in enumerate(column_slab(ffn_w1[layer], (i + 2) * BLK)):
                        n = first[1] + 8 + q
                        sp.wait_ge(lo_split, n - NRAW + 1 + i * 8)
                        dst = raw[:, n % NRAW, :].rearrange("p (k n) -> p k n", k=2)
                        sp.dma_start(dst, src).then_inc(raw_in[n % NRAW], 16)
            sp.wait_ge(out_done, 16 * TT)

        @block.gpsimd
        def _(pool):
            pool.memset(ident[:, :], 0.0).then_inc(ident_step, 1)
            pool.wait_ge(ident_step, 1)
            pool.affine_select(out=ident[:, :], in_=ident[:, :], compare_op=ALU.not_equal, fill=1.0, base=0,
                               pattern=[[-1, P]], channel_multiplier=1).then_inc(ident_step, 1)
            pool.wait_ge(param_in, 16 * 7)
            pool.affine_select(out=ws_n, in_=ws_n, compare_op=ALU.is_ge, fill=0.0, base=0,
                               pattern=[[0, 4], [-1, P]], channel_multiplier=1).then_inc(ident_step, 1)

            def split_low(slab, piece, count, i=0):
                for q in range(count):
                    n = piece + q
                    pool.wait_ge(hi_split, n + 1 + i * 8)
                    s = slice(q * PIECE, (q + 1) * PIECE)
                    pool.tensor_tensor(w_lo[:, slab % 2, s], raw[:, n % NRAW, :], w_hi[:, slab % 2, s].bitcast(F32),
                                       ALU.subtract).then_inc(lo_split, 1)

            split_low(0, 0, 4)

            def stage(st):
                if st.first and st.cur + 1 < n_slabs:
                    if st.step:
                        split_low(st.cur + 1, st.piece, 4, st.i)
                    else:
                        nxt = slabs[st.cur + 1]
                        split_low(st.cur + 1, st.piece, 5 if nxt and nxt[0][0] == "gate" else 4)
                if st.kind == "alpha":
                    pool.wait_ge(a_full, st.ga)
                    for k in range(HT):
                        t = st.half * HT + k
                        pool.tensor_scalar(resid[:, t, :], resid[:, t, :], ALPHA, 1.0, ALU.mult, ALU.mult)\
                            .then_inc(acc_ready, 1)
                if st.kind == "stats" and st.half == 0 and st.ln % 2 == 0:
                    pool.wait_ge(gb_in, 32 * (st.ln + 2))
                    pool.tensor_scalar(gb_rows[:, :, :], gb_rows[:, :, :], ALPHA, 1.0, ALU.mult, ALU.mult)\
                        .then_inc(gb_scaled, 1)
                if st.kind == "affine":
                    for k in range(HT):
                        t = st.half * HT + k
                        pool.wait_ge(gained, st.ln * TT + t + 1)
                        pool.tensor_tensor(resid[:, t, :], resid[:, t, :], gb_rows[:, 1, :], ALU.add)\
                            .then_inc(acc_ready, 1)

            walk(stage, pool.Fori)

        @block.scalar
        def _(act):
            def split_high(slab, piece, count, i=0, end=None):
                for q in range(count):
                    n = piece + q
                    if end is not None and q == 0:
                        act.wait_ge(sem_of[end[0]], end[1])
                    act.wait_ge(raw_in[n % NRAW], 16 * (n // NRAW + 1) + i * 32)
                    act.copy(w_hi[:, slab % 2, q * PIECE:(q + 1) * PIECE], raw[:, n % NRAW, :]).then_inc(hi_split, 1)

            split_high(0, 0, 4)

            def stage(st):
                if st.first and st.cur + 1 < n_slabs:
                    end = None
                    if st.cur >= 1:
                        name, value = slab_end[st.cur - 1]
                        end = (name, st.later(value, name))
                    if st.step:
                        split_high(st.cur + 1, st.piece, 4, st.i, end)
                    else:
                        nxt = slabs[st.cur + 1]
                        split_high(st.cur + 1, st.piece, 5 if nxt and nxt[0][0] == "gate" else 4, 0, end)
                if st.kind == "consts":
                    act.wait_ge(a_full, 1)
                    act.copy(cols[:, :], bank_a[0][:, 0:ROWS]).then_inc(moved, 1)
                    act.wait_ge(a_full, 2)
                    act.copy(ws_t[:, :, :], bank_a[1][:, :].rearrange("p (h t) -> p h t", h=4)).then_inc(moved, 1)
                if st.kind in ("turn", "turn_p", "ffn", "lin"):
                    for k in range(len(st.js) if st.kind == "turn" else 2):
                        act.wait_ge(a_full, st.n("ga", k + 1))
                        if st.unit + k >= NTMP:
                            act.wait_ge(unit_lo, st.n("unit", k - NTMP + 1))
                        dst = tmp[:, (st.unit + k) % NTMP, :]
                        src = bank_a[(st.ga + k) % RING][:, :]
                        if st.kind == "ffn":
                            act.activation(dst, src, ACT.Relu).then_inc(act_value, 1)
                        elif st.kind == "lin":
                            g = ROW_POOL + st.blk * BT + k
                            act.activation(dst, src, ACT.Copy, scale=cols[:, g:g + 1]).then_inc(act_value, 1)
                        elif st.kind == "turn" and st.source == "ln":
                            g = ROW_G[st.ln % 2] + st.ln // 2 * KT + st.js[k]
                            b = ROW_B[st.ln % 2] + st.ln // 2 * KT + st.js[k]
                            act.activation(dst, src, ACT.Identity, scale=cols[:, g:g + 1], bias=cols[:, b:b + 1])\
                                .then_inc(act_value, 1)
                        else:
                            act.copy(dst, src).then_inc(act_value, 1)
                if st.kind in ("u", "a", "c"):
                    if st.half == 0 and (st.kind != "a" or st.g == 0):
                        act.wait_ge(unit_lo, st.unit)
                    for k in ([st.g] if st.kind == "a" else range(BT)):
                        j = 0 if st.kind == "a" else k
                        act.wait_ge(a_full, st.ga + j + 1)
                        s = slice(st.half * HALF, (st.half + 1) * HALF)
                        if st.kind == "a":
                            dst = a_t[:, k, PAD + st.half * HALF:PAD + (st.half + 1) * HALF]
                        else:
                            dst = (u_t if st.kind == "u" else cv)[:, k, s]
                        act.copy(dst, bank_a[(st.ga + j) % RING][:, :]).then_inc(moved, 1)
                if st.kind in ("vln", "stats"):
                    m = st.half if st.kind == "vln" else 2 + 2 * st.ln + st.half
                    act.wait_ge(var_ready, m + 1)
                    act.activation(std[:, :], var_eps[:, :], ACT.Sqrt).then_inc(std_ready, 1)
                    if st.kind == "stats":
                        act.wait_ge(norm_ready, 2 * st.ln + st.half + 1)
                        for k in range(2):
                            t = st.half * HT + k
                            act.activation(resid[:, t, :], resid[:, t, :], ACT.Identity, scale=rstd[:, k:k + 1],
                                           bias=neg_mean[:, k:k + 1]).then_inc(xn_act, 1)
                if st.kind == "gate":
                    for k, t in enumerate(st.tiles):
                        act.wait_ge(b_full, st.gb + k + 1)
                        if st.xnew + k >= 2:
                            act.wait_ge(x_new, st.xnew + k - 1)
                        else:
                            act.wait_ge(a_full, st.ga)
                        act.activation(sig[:, (st.xnew + k) % 2, :], bank_b[(st.gb + k) % RING][:, 0:BLK],
                                       ACT.Sigmoid).then_inc(sig_ready, 1)

            walk(stage, act.Fori)

        @block.vector
        def _(dve):
            steps = [0]

            def link(ins):
                steps[0] += 1
                ins.then_inc(ln_step, 1)
                dve.wait_ge(ln_step, steps[0])

            for t in range(PAD):
                dve.memset(inv_cnt[:, t:t + 1], 1.0 / (t + 1)).then_inc(dve_const, 1)
            windows = [0]
            convs = [0]

            def target(st, k):
                s = slice(st.half * HALF, (st.half + 1) * HALF)
                if st.kind == "turn":
                    return xt_hi[:, st.js[k], s], xt_lo[:, st.js[k], s]
                return hid_hi[:, k, s], hid_lo[:, k, s]

            def put_high(st, k):
                dve.tensor_copy(target(st, k)[0], tmp[:, (st.unit + k) % NTMP, :]).then_inc(unit_hi, 1)

            def put_low(st, k):
                dve.wait_ge(unit_hi, st.n("unit", k + 1))
                hi, lo = target(st, k)
                dve.tensor_tensor(lo, tmp[:, (st.unit + k) % NTMP, :], hi.bitcast(F32), ALU.subtract)\
                    .then_inc(unit_lo, 1)

            def statistics(width, m):
                for k in range(HT):
                    ins = dve.bn_aggr(mean_var[:, k, :], bn6[:, k, 0:6 * (width // 512)])
                link(ins)
                dve.tensor_scalar(var_eps[:, :], mean_var[:, :, 1], EPS, None, ALU.add).then_inc(var_ready, 1)
                dve.wait_ge(std_ready, m + 1)
                link(dve.reciprocal(rstd[:, :], std[:, :]))
                link(dve.tensor_tensor(newton[:, :], rstd[:, :], rstd[:, :], ALU.mult))
                link(dve.tensor_tensor(newton[:, :], newton[:, :], var_eps[:, :], ALU.mult))
                link(dve.tensor_scalar(newton[:, :], newton[:, :], -0.5, 1.5, ALU.mult, ALU.add))
                link(dve.tensor_tensor(rstd[:, :], rstd[:, :], newton[:, :], ALU.mult))

            def stage(st):
                if st.kind in ("turn", "turn_p", "lin"):
                    count = len(st.js) if st.kind == "turn" else 2
                    for k in range(count + 1):
                        if k < count:
                            dve.wait_ge(act_value, st.n("aval", k + 1))
                            put_high(st, k)
                        if k >= 1:
                            put_low(st, k - 1)

                if st.kind == "ffn":
                    for k in range(2):
                        dve.wait_ge(act_value, st.n("aval", k + 1))
                        t = tmp[:, (st.unit + k) % NTMP, :]
                        dve.tensor_tensor(t, t, t, ALU.mult).then_inc(dve_value, 1)
                        dve.wait_ge(dve_value, st.n("dval", k + 1))
                        put_high(st, k)
                        put_low(st, k)

                if st.kind == "out":
                    dve.wait_ge(acc_ready, st.accd)
                    for k in range(2 * len(st.tiles)):
                        t, n = st.tiles[k // 2], k % 2
                        r = resid[:, t, n * HALF:(n + 1) * HALF]
                        dve.wait_ge(b_full, st.n("gb", k + 1))
                        dve.wait_ge(b_free, st.n("gb", k - 7))
                        dve.tensor_tensor(r, r, bank_b[(st.gb + k) % RING][:, :], ALU.add).then_inc(b_free, 1)

                if st.kind == "v":
                    for k, t in enumerate(st.tiles):
                        dve.wait_ge(b_full, st.gb + k + 1)
                        dve.tensor_copy(v_n[:, t, st.col * BLK:(st.col + 1) * BLK],
                                        bank_b[(st.gb + k) % RING][:, 0:BLK]).then_inc(b_free, 1)

                if st.kind == "vln":
                    if st.half == 0:
                        dve.wait_ge(gb_in, 32)
                    dve.wait_ge(b_free, st.gb)
                    for k in range(HT):
                        ins = dve.bn_stats(bn6[:, k, 0:6], v_n[:, st.half * HT + k, :])
                    link(ins)
                    statistics(WIDTH, st.half)
                    for k in range(HT):
                        v = v_n[:, st.half * HT + k, :]
                        ins = dve.tensor_scalar(v, v, mean_var[:, k, 0:1], rstd[:, k:k + 1], ALU.subtract, ALU.mult)
                    link(ins)
                    for k in range(HT):
                        v = v_n[:, st.half * HT + k, :]
                        ins = dve.tensor_tensor(v, v, gb_rows[:, 0, 0:WIDTH], ALU.mult)
                    link(ins)
                    for k in range(HT):
                        v = v_n[:, st.half * HT + k, :]
                        dve.tensor_tensor(v, v, gb_rows[:, 1, 0:WIDTH], ALU.add).then_inc(vn_ready, 1)

                if st.kind == "stats":
                    dve.wait_ge(b_free, st.gb)
                    for k in range(HT):
                        for n in range(2):
                            ins = dve.bn_stats(bn6[:, k, 6 * n:6 * n + 6],
                                               resid[:, st.half * HT + k, n * HALF:(n + 1) * HALF])
                    if 2 * st.ln + st.half:
                        dve.wait_ge(xn_act, 2 * (2 * st.ln + st.half))
                        dve.wait_ge(xn_dve, 2 * (2 * st.ln + st.half))
                    link(ins)
                    statistics(D, 2 + 2 * st.ln + st.half)
                    dve.scalar_tensor_tensor(out=neg_mean[:, :], in0=mean_var[:, :, 0], scalar=-1.0, in1=rstd[:, :],
                                             op0=ALU.mult, op1=ALU.mult).then_inc(norm_ready, 1)
                    for k in range(2, HT):
                        r = resid[:, st.half * HT + k, :]
                        dve.tensor_scalar(r, r, mean_var[:, k, 0:1], rstd[:, k:k + 1], ALU.subtract, ALU.mult)\
                            .then_inc(xn_dve, 1)

                if st.kind == "affine":
                    if st.half == 0:
                        dve.wait_ge(gb_in, 32 * (st.ln + 2))
                        if st.ln % 2 == 0:
                            dve.wait_ge(gb_scaled, st.ln // 2 + 1)
                    dve.wait_ge(a_full, st.ga)
                    for k in range(HT):
                        r = resid[:, st.half * HT + k, :]
                        dve.tensor_tensor(r, r, gb_rows[:, 0, :], ALU.mult).then_inc(gained, 1)

                if st.kind == "mix":
                    if st.half == 0 and st.blk == 0:
                        dve.wait_ge(late_in, 32)
                    for k in range(2):
                        t = tmp[:, (st.unit + k) % NTMP, :]
                        bias = sgu_b[:, st.blk * BT + k, :].unsqueeze(1).to_broadcast([P, HT, P])
                        dve.wait_ge(a_full, st.ga + k + 1)
                        dve.wait_ge(unit_lo, st.unit + k - NTMP + 1)
                        dve.tensor_tensor(t.rearrange("p (c t) -> p c t", c=HT),
                                          bank_a[(st.ga + k) % RING][:, :].rearrange("p (c t) -> p c t", c=HT),
                                          bias, ALU.add).then_inc(mix_read, 1)
                        dve.wait_ge(mix_read, st.mixg + k + 1)
                        dve.wait_ge(moved, st.moved)
                        dve.tensor_tensor(t, t, u_t[:, k, st.half * HALF:(st.half + 1) * HALF], ALU.mult)\
                            .then_inc(dve_value, 1)
                        dve.wait_ge(dve_value, st.dval + k + 1)
                        put_high(st, k)
                        put_low(st, k)

                if st.kind == "a":
                    g = st.blk * BT + st.g
                    w = WINDOWS[g]
                    k = st.g

                    def wlink(ins):
                        windows[0] += 1
                        ins.then_inc(window_step, 1)
                        dve.wait_ge(window_step, windows[0])

                    if st.half == 0:
                        dve.wait_ge(unit_lo, st.unit)
                        wlink(dve.memset(a_t[:, k, 0:PAD], 0.0))
                    dve.wait_ge(moved, st.moved + 1)
                    src, o, length, history = a_t[:, k, :], PAD + st.half * HALF, 1, w - 2
                    b = 0
                    while length < w:
                        dst = win[:, b, :]
                        n = HALF + history
                        wlink(dve.tensor_tensor(dst[:, PAD - history:PAD + HALF], src[:, o - history:o + HALF],
                                                src[:, o - history - length:o + HALF - length], ALU.add))
                        src, o, b = dst, PAD, 1 - b
                        length *= 2
                        history -= length
                    a = a_t[:, k, PAD + st.half * HALF:PAD + (st.half + 1) * HALF]
                    q = pooled[:, k, st.half * HALF:(st.half + 1) * HALF]
                    wlink(dve.scalar_tensor_tensor(out=q, in0=src[:, PAD:PAD + HALF], scalar=1.0 / w, in1=a,
                                                   op0=ALU.mult, op1=ALU.subtract))
                    if st.half == 0:
                        dve.wait_ge(dve_const, PAD)
                        other = win[:, b, 0:PAD]
                        wlink(dve.scalar_tensor_tensor(out=other, in0=inv_cnt[:, :], scalar=1.0 / w,
                                                       in1=src[:, PAD:2 * PAD], op0=ALU.max, op1=ALU.mult))
                        wlink(dve.tensor_tensor(q[:, 0:PAD], other, a[:, 0:PAD], ALU.subtract))

                if st.kind == "h":
                    def clink(ins):
                        convs[0] += 1
                        ins.then_inc(conv_step, 1)
                        dve.wait_ge(conv_step, convs[0])

                    if st.half == 0 and st.blk == 0:
                        dve.wait_ge(unit_lo, st.unit)
                        clink(dve.memset(z[:, :, 0:2], 0.0))
                    for k in range(2):
                        s = slice(st.half * HALF, (st.half + 1) * HALF)
                        o = 2 + st.half * HALF
                        tile = st.blk * BT + k
                        tap = [cols[:, ROW_CONV + j * KT + tile:ROW_CONV + j * KT + tile + 1] for j in range(3)]
                        dve.wait_ge(a_full, st.ga + k + 1)
                        dve.wait_ge(moved, st.moved)
                        dve.tensor_tensor(z[:, k, o:o + HALF], bank_a[(st.ga + k) % RING][:, :], cv[:, k, s],
                                          ALU.mult).then_inc(z_ready, 1)
                        dve.wait_ge(z_ready, st.conv + k + 1)
                        clink(dve.tensor_scalar(cv[:, k, s], z[:, k, o:o + HALF], tap[2], None, ALU.mult))
                        clink(dve.scalar_tensor_tensor(out=cv[:, k, s], in0=z[:, k, o - 1:o - 1 + HALF],
                                                       scalar=tap[1], in1=cv[:, k, s], op0=ALU.mult, op1=ALU.add))
                        clink(dve.scalar_tensor_tensor(out=cv[:, k, s], in0=z[:, k, o - 2:o - 2 + HALF],
                                                       scalar=tap[0], in1=cv[:, k, s], op0=ALU.mult, op1=ALU.add))

                if st.kind == "bgate":
                    for k in range(2):
                        t = tmp[:, (st.unit + k) % NTMP, :]
                        dve.wait_ge(a_full, st.ga + k + 1)
                        dve.wait_ge(unit_lo, st.unit + k - NTMP + 1)
                        dve.tensor_tensor(t, bank_a[(st.ga + k) % RING][:, :],
                                          cv[:, k, st.half * HALF:(st.half + 1) * HALF], ALU.mult)\
                            .then_inc(dve_value, 1)
                        dve.wait_ge(dve_value, st.dval + k + 1)
                        put_high(st, k)
                        put_low(st, k)

                if st.kind == "gate":
                    for k, t in enumerate(st.tiles):
                        c = slice(st.col * BLK, (st.col + 1) * BLK)
                        s = sig[:, (st.xnew + k) % 2, :]
                        dve.wait_ge(sig_ready, st.xnew + k + 1)
                        dve.wait_ge(acc_ready, st.accd - HT + k + 1 if st.col == 0 else st.accd)
                        dve.tensor_tensor(s, s, bank_b[(st.gb + k) % RING][:, BLK:2 * BLK], ALU.mult)\
                            .then_inc(b_free, 1)
                        dve.wait_ge(b_free, st.gb + k + 1)
                        dve.tensor_tensor(resid[:, t, c], resid[:, t, c], s, ALU.add).then_inc(x_new, 1)

            walk(stage, dve.Fori)

        @block.tensor
        def _(pe):
            def bank_is_free_a(st, k):
                g = st.ga + k
                if g >= RING:
                    name, value = freed[g - RING]
                    pe.wait_ge(sem_of[name], st.later(value, name))
                return bank_a[g % RING]

            def bank_is_free_b(st, k):
                if st.gb + k >= RING:
                    pe.wait_ge(b_free, st.n("gb", k - RING + 1))
                return bank_b[(st.gb + k) % RING]

            def product(dst, stationary, moving, first, last):
                (s_hi, s_lo), (m_hi, m_lo) = stationary, moving
                pe.matmul(dst, s_hi, m_hi, start=first, stop=False)
                pe.matmul(dst, s_hi, m_lo, start=False, stop=False)
                return pe.matmul(dst, s_lo, m_hi, start=False, stop=last)

            def xt(j, s):
                return xt_hi[:, j, s], xt_lo[:, j, s]

            def hid(j, s):
                return hid_hi[:, j, s], hid_lo[:, j, s]

            def slot(st, at, count):
                s = st.cur % 2
                return w_hi[:, s, at:at + count], w_lo[:, s, at:at + count]

            def stage(st):
                if st.first:
                    pe.wait_ge(lo_split, st.n("piece"))
                if st.kind == "consts":
                    pe.wait_ge(ident_step, 3)
                    pe.transpose(bank_a[0][:, 0:ROWS], rows_n, ident[0:ROWS, 0:ROWS]).then_inc(a_full, 1)
                    for h in range(4):
                        ins = pe.transpose(bank_a[1][:, h * P:(h + 1) * P], ws_n[:, h, :], ident[:, :])
                    ins.then_inc(a_full, 1)
                if st.kind == "turn":
                    if st.source == "input":
                        pe.wait_ge(x_in[st.half], 16 * HT)
                    elif st.source == "ln":
                        pe.wait_ge(xn_act, 2 * (2 * st.ln + st.half + 1))
                        pe.wait_ge(xn_dve, 2 * (2 * st.ln + st.half + 1))
                    else:
                        pe.wait_ge(x_new, 3 * TT + (st.half + 1) * HT)
                    for k, j in enumerate(st.js):
                        dst = bank_is_free_a(st, k)
                        for t in range(HT):
                            ins = pe.transpose(dst[:, t * P:(t + 1) * P],
                                               resid[:, st.half * HT + t, j * P:(j + 1) * P], ident[:, :])
                        ins.then_inc(a_full, 1)
                if st.kind == "turn_p":
                    pe.wait_ge(p_in, 16 * (st.layer + 1))
                    for k in range(2):
                        dst = bank_is_free_a(st, k)
                        for t in range(HT):
                            ins = pe.transpose(dst[:, t * P:(t + 1) * P],
                                               p_n[:, st.half * HT + t, k * P:(k + 1) * P], ident[:, :])
                        ins.then_inc(a_full, 1)
                if st.kind in ("ffn", "u", "a", "c", "h", "bgate"):
                    pe.wait_ge(unit_lo, st.need_x[st.half])
                    for j, k in enumerate([st.g] if st.kind == "a" else range(BT)):
                        dst = bank_is_free_a(st, j)[:, :]
                        for q in range(KT):
                            ins = product(dst, slot(st, q * BLK + k * P, P),
                                          xt(q, slice(st.half * HALF, (st.half + 1) * HALF)), q == 0, q == KT - 1)
                        ins.then_inc(a_full, 1)
                if st.kind == "out":
                    for k in range(2 * len(st.tiles)):
                        t, n = st.tiles[k // 2], k % 2
                        if k == 0 or t == HT:
                            pe.wait_ge(unit_lo, st.later(st.need_h[t // HT], "unit"))
                        dst = bank_is_free_b(st, k)[:, :]
                        for q in range(BT):
                            ins = product(dst, hid(q, slice(t * P, (t + 1) * P)), slot(st, q * D + n * HALF, HALF),
                                          q == 0, q == BT - 1)
                        ins.then_inc(b_full, 1)
                if st.kind == "v":
                    pe.wait_ge(unit_lo, st.need_x[st.tiles[0] // HT])
                    for k, t in enumerate(st.tiles):
                        dst = bank_is_free_b(st, k)[:, 0:BLK]
                        for q in range(KT):
                            ins = product(dst, xt(q, slice(t * P, (t + 1) * P)), slot(st, q * BLK, BLK),
                                          q == 0, q == KT - 1)
                        ins.then_inc(b_full, 1)
                if st.kind == "gate":
                    h = st.tiles[0] // HT
                    pe.wait_ge(unit_lo, max(st.need_x[h] if st.col < 3 else 0, st.need_h[h]))
                    for k, t in enumerate(st.tiles):
                        bank = bank_is_free_b(st, k)
                        s = slice(t * P, (t + 1) * P)
                        for q in range(KT):
                            product(bank[:, 0:BLK], xt(q, s), slot(st, q * BLK, BLK), q == 0, q == KT - 1)
                        for q in range(PLE // P):
                            ins = product(bank[:, BLK:2 * BLK], hid(q, s), slot(st, KT * BLK + q * BLK, BLK),
                                          q == 0, q == PLE // P - 1)
                        ins.then_inc(b_full, 1)
                if st.kind == "mix":
                    pe.wait_ge(vn_ready, HT * (st.half + 1))
                    pe.wait_ge(moved, 2)
                    for k in range(2):
                        head = st.blk * BT + k
                        dst = bank_is_free_a(st, k)
                        for c in range(HT):
                            ins = pe.matmul(dst[:, c * P:(c + 1) * P],
                                            v_n[:, st.half * HT + c, head * P:(head + 1) * P], ws_t[:, head, :],
                                            start=True, stop=True)
                        ins.then_inc(a_full, 1)
                if st.kind == "lin":
                    pe.wait_ge(window_step, window_steps(st))
                    pe.wait_ge(late_in, 32)
                    for k in range(2):
                        pe.matmul(bank_is_free_a(st, k)[:, :], pool_w[:, st.blk * BT + k, :],
                                  pooled[:, k, st.half * HALF:(st.half + 1) * HALF], start=True, stop=True)\
                            .then_inc(a_full, 1)

            def window_steps(st):
                def steps_of(half, g):
                    levels = WINDOWS[g].bit_length() - 1
                    return levels + (4 if half == 0 else 1)
                order = [(b, h, g) for b in range(2) for h in range(2) for g in range(BT)]
                upto = order.index((st.blk, st.half, BT - 1))
                return sum(steps_of(h, b * BT + g) for b, h, g in order[:upto + 1])

            walk(stage, pe.Fori)


_INS = ["x", "p", "ev_w_in", "ev_pool_w", "ev_pool_scale", "ev_sgu_ln_g", "ev_sgu_ln_b", "ev_sgu_w", "ev_sgu_b",
        "ev_w_out", "od_w_in", "od_conv_w", "od_w_out", "ln1_g", "ln1_b", "ffn_w1", "ffn_w2", "ln2_g", "ln2_b",
        "ple_gate_w", "ple_w"]


def kernel(**inputs):
    import numpy as _np
    import concourse.bacc as _bacc
    from concourse import mybir as _mybir
    from concourse.bass_utils import run_bass_kernel_spmd as _run

    nc = _bacc.Bacc("TRN2", target_bir_lowering=False, num_devices=1)
    arrays, args = {}, []
    for name in _INS:
        a = _np.ascontiguousarray(inputs[name])
        arrays[f"in_{name}_dram"] = a
        args.append(nc.dram_tensor(f"in_{name}_dram", a.shape, _mybir.dt.from_np(a.dtype), kind="ExternalInput").ap())
    args.append(nc.dram_tensor("out_dram", (1, SEQ, D), F32, kind="ExternalOutput").ap())
    trunk(nc, *args)
    r = _run(nc, [arrays], core_ids=[0])
    return r.results[0]["out_dram"]
```

```python
from contextlib import ExitStack

import concourse.bass as bass
from concourse import mybir

P = 128
F32 = mybir.dt.float32
F32R = mybir.dt.float32r
ALU = mybir.AluOpType
ACT = mybir.ActivationFunctionType

SEQ = 1024
D = 1024
KT = D // P
TT = SEQ // P
HALF = 512
HT = HALF // P
BLK = 256
BT = BLK // P
WIDTH = 512
FF = 4 * D
FFN_BLOCKS = FF // BLK
OD_BLOCKS = D // BLK
PLE = 256
PIECE = 512
NRAW = 4
NTMP = 4
RING = 4
WINDOWS = (2, 4, 8, 16)
PAD = 16
EPS = 1e-5
ALPHA = 4.0 ** 0.25

ROW_G = (0, 32)
ROW_B = (16, 48)
ROW_POOL = 64
ROW_CONV = 68
ROWS = 92


class Stage:

    def __init__(self, kind, at, half=0, blk=0, g=0, js=(), tiles=(), source=None, layer=0, ln=None, col=0,
                 first=False, cur=0, body=(), trips=0, ring="A", inner=(), nested=False, paced=False, sums=None,
                 early=False, split_next=None):
        self.kind = kind
        self.at = dict(at)
        self.i = 0
        self.step = {}
        self.half, self.blk, self.g, self.js, self.tiles = half, blk, g, js, tiles
        self.source, self.layer, self.ln, self.col = source, layer, ln, col
        self.first, self.cur = first, cur
        self.body, self.trips = body, trips
        self.ring = ring
        self.inner, self.nested = inner, nested
        self.paced = paced
        self.split_next = first if split_next is None else split_next
        self.early = early
        self.sums = sums
        self.turned = [None, None]
        self.need_x, self.need_h = [0, 0], [0, 0]
        self.ga, self.gb, self.unit = at["ga"], at["gb"], at["unit"]
        self.moved, self.mixg, self.conv, self.dval = at["moved"], at["mixg"], at["conv"], at["dval"]
        self.bread, self.sq = at["bread"], at["sq"]
        self.xnew, self.accd, self.piece = at["xnew"], at["accd"], at["piece"]

    def n(self, name, k=0):
        v = self.at[name] + k
        return v + self.i * self.step[name] if name in self.step else v

    def later(self, value, name):
        return value + self.i * self.step[name] if name in self.step else value


COUNTS = ("ga", "gb", "unit", "aval", "dval", "moved", "conv", "xnew", "accd", "slab", "piece", "bread", "sq")
ADDS = {
    "consts": dict(ga=2, moved=2),
    "turn_p": dict(ga=2, unit=2, aval=2),
    "u": dict(ga=2, moved=2),
    "mix": dict(ga=2, unit=2, dval=2),
    "a": dict(ga=1, moved=1),
    "lin": dict(ga=2, unit=2, aval=2),
    "c": dict(ga=2, moved=2),
    "h": dict(ga=2, conv=2),
    "bgate": dict(ga=2, unit=2, dval=2),
    "ffn": dict(ga=2, unit=2, aval=2, dval=2),
    "alpha": dict(accd=HT),
    "affine": dict(accd=HT),
    "vln": {}, "stats": {},
}
FREED_BY = dict(consts="moved", turn="aval", turn_p="aval", u="moved", mix="mixg", a="moved", lin="aval", c="moved",
                h="conv", bgate="dval", ffn="aval", out="bread", v="bread", gate="bread")


def make_plan():
    at = dict.fromkeys(COUNTS, 0)
    at["mixg"] = 0
    plan, freed, slab_end, slabs = [], {"A": [], "B": []}, [], []
    need = dict(xu=[0, 0], hu=[0, 0])
    turned = [None, None]
    where = [plan]

    def add(kind, slab=None, last=False, **args):
        if slab is not None:
            slabs.append((slab, at["piece"]))
            at["slab"] += 1
            at["piece"] += 5 if slab[0] == "gate" else 4
        st = Stage(kind, at, first=slab is not None, cur=at["slab"] - 1, **args)
        st.need_x, st.need_h, st.turned = list(need["xu"]), list(need["hu"]), list(turned)
        adds = dict(ADDS.get(kind, {}))
        if kind in ("out", "gate", "v"):
            adds["gb"] = adds["bread"] = len(args["tiles"]) * (2 if kind == "out" else 1)
            if kind == "gate":
                adds["xnew"] = len(args["tiles"])
            if args.get("sums") is not None:
                adds["sq"] = len(args["tiles"])
        if kind == "turn":
            adds.update(ga=len(args["js"]), unit=len(args["js"]), aval=len(args["js"]))
        if args.get("ring") == "B":
            adds["gb"] = adds.pop("ga")
        if kind == "mix":
            adds["mixg"] = 2
        by = FREED_BY.get(kind)
        for ring, name in (("A", "ga"), ("B", "gb")):
            for k in range(adds.get(name, 0)):
                freed[ring].append((by, at[by] + k + 1))
        for name, k in adds.items():
            at[name] += k
        if kind == "turn":
            need["xu"][st.half] = at["unit"]
            turned[st.half] = ("gb", at["gb"]) if st.ring == "B" else ("ga", at["ga"])
        if kind in ("turn_p", "mix", "lin", "bgate", "ffn"):
            need["hu"][st.half] = at["unit"]
        if last:
            slab_end.append(("ga", at["ga"]) if kind in ("u", "a", "c", "h", "bgate", "ffn") else ("gb", at["gb"]))
        where[-1].append(st)
        return st

    lo, hi = list(range(HT)), list(range(HT, TT))

    def turns(source, half, js, layer=0, ln=None, ring="A", nested=False, early=False):
        return add("turn", source=source, half=half, js=js, layer=layer, ln=ln, ring=ring, nested=nested,
                   early=early)

    def last_half(kind, source, p=False, layer=0, ln=None, **args):
        st = add(kind, tiles=hi, last=True, layer=layer, **args)
        st.inner = [turns(source, 0, [0, 1, 2, 3], ln=ln, nested=True, early=True)]
        turns(source, 0, [4, 5, 6, 7], ln=ln, ring="B")
        if p:
            add("turn_p", half=0, layer=layer)
        if ln is not None:
            add("stats", half=1, ln=ln)

    def block_out(rows, ln=None, layer=0, p=False):
        add("out", slab=rows, tiles=lo, sums=ln)
        if ln is None:
            add("out", tiles=hi, last=True)
            return
        add("stats", half=0, ln=ln)
        last_half("out", "ln", p=p, layer=layer, ln=ln, sums=ln)

    def feature_halves(kind, slab, source, ln=None, **args):
        scale = "alpha" if ln is None else "affine"
        add(scale, half=0, ln=ln)
        turn = turns(source, 1, list(range(KT)), ln=ln, ring="B", nested=True)
        add(kind, slab=slab, half=0, paced=True, inner=[turn], **args)
        add(scale, half=1, ln=ln)
        add(kind, half=1, paced=True, last=True, **args)

    def token_halves(kind, slab, source, ln=None, p=False, layer=0, **args):
        add(kind, slab=slab, tiles=[0, 1], paced=True, layer=layer, split_next=False, **args)
        inner = [turns(source, 1, list(range(KT)), ln=ln, nested=True)]
        if p:
            inner.append(add("turn_p", half=1, layer=layer, nested=True))
        add(kind, tiles=[2, 3], inner=inner, layer=layer, split_next=True, **args)
        if source == "input":
            add("alpha", half=0)
            add("alpha", half=1)
        add(kind, tiles=[4, 5], paced=True, layer=layer, **args)
        add(kind, tiles=[6, 7], last=True, layer=layer, **args)

    def ffn(layer):
        feature_halves("ffn", ("w1", layer, 0), "ln", ln=2 * layer)
        block_out(("w2", layer, 0))
        body, before = [], dict(at)
        where.append(body)
        add("ffn", slab=("w1", layer, "loop"), half=0)
        add("ffn", half=1, last=True)
        block_out(("w2", layer, "loop"))
        where.pop()
        trips = FFN_BLOCKS - 2
        step = {k: at[k] - before[k] for k in at if at[k] != before[k]}
        for st in body:
            st.step = step
        loop = Stage("loop", before, body=body, trips=trips, layer=layer)
        where[-1].append(loop)
        for k, v in step.items():
            at[k] += v * (trips - 1)
        need["hu"] = [x + step["unit"] * (trips - 1) for x in need["hu"]]
        ls = step["slab"]
        for t in range(1, trips):
            for ring, count in (("A", step["ga"]), ("B", step["gb"])):
                for name, v in freed[ring][-count:]:
                    freed[ring].append((name, v + step[name]))
            for name, v in slab_end[-ls:]:
                slab_end.append((name, v + step[name]))
        for t in range(1, trips):
            slabs.extend([None] * ls)
        add("ffn", slab=("w1", layer, FFN_BLOCKS - 1), half=0)
        add("ffn", half=1, last=True)
        block_out(("w2", layer, FFN_BLOCKS - 1), ln=2 * layer + 1, layer=layer, p=True)

    def gates(layer):
        for c in range(4):
            slab = ("gate", layer, c)
            if c == 0:
                token_halves("gate", slab, "ln", ln=2 * layer + 1, p=True, layer=layer, col=c)
                continue
            add("gate", slab=slab, tiles=lo, col=c, layer=layer)
            if c == 3 and layer == 0:
                last_half("gate", "gate", layer=layer, col=c)
            else:
                add("gate", tiles=hi, col=c, layer=layer, last=True)

    turns("input", 0, list(range(KT)))
    token_halves("v", ("ev", 4 * BLK), "input")
    add("consts")
    add("v", slab=("ev", 5 * BLK), tiles=lo, col=1)
    add("vln", half=0)
    add("v", tiles=hi, col=1, last=True)
    add("vln", half=1)
    for blk in range(2):
        add("u", slab=("ev", WIDTH + blk * BLK), half=0, blk=blk)
        add("mix", half=0, blk=blk)
        add("u", half=1, blk=blk, last=True)
        add("mix", half=1, blk=blk)
        block_out(("ev_out", WIDTH + blk * BLK))
    for blk in range(2):
        add("a", slab=("ev", blk * BLK), half=0, blk=blk, g=0)
        add("a", half=0, blk=blk, g=1)
        add("a", half=1, blk=blk, g=0)
        add("lin", half=0, blk=blk)
        add("a", half=1, blk=blk, g=1, last=True)
        rows, sums = ("ev_out", blk * BLK), 0 if blk == 1 else None
        add("out", slab=rows, tiles=[0, 1, 2], sums=sums)
        add("lin", half=1, blk=blk)
        add("out", tiles=[3], sums=sums)
        if blk == 0:
            add("out", tiles=hi, last=True)
    add("stats", half=0, ln=0)
    last_half("out", "ln", ln=0, sums=0)
    ffn(0)
    gates(0)
    for blk in range(OD_BLOCKS):
        if blk == 0:
            feature_halves("c", ("od", D), "gate")
        else:
            add("c", slab=("od", D + blk * BLK), half=0, blk=blk)
            add("c", half=1, blk=blk, last=True)
        add("h", slab=("od", 2 * D + blk * BLK), half=0, blk=blk)
        add("h", half=1, blk=blk, last=True)
        add("bgate", slab=("od", blk * BLK), half=0, blk=blk)
        add("bgate", half=1, blk=blk, last=True)
        block_out(("od_out", blk * BLK), ln=2 if blk == OD_BLOCKS - 1 else None)
    ffn(1)
    gates(1)
    return plan, freed, slab_end, slabs, dict(at)


def trunk(nc, x, p, ev_w_in, ev_pool_w, ev_pool_scale, ev_sgu_ln_g, ev_sgu_ln_b, ev_sgu_w, ev_sgu_b, ev_w_out,
          od_w_in, od_conv_w, od_w_out, ln1_g, ln1_b, ffn_w1, ffn_w2, ln2_g, ln2_b, ple_gate_w, ple_w, out):
    plan, freed, slab_end, slabs, total = make_plan()
    n_slabs = total["slab"]

    x_v = x[0].rearrange("(t p) d -> p t d", p=P)
    out_v = out[0].rearrange("(t p) d -> p t d", p=P)

    with ExitStack() as ctx:
        def sb(name, shape, dt=F32):
            return ctx.enter_context(nc.sbuf_tensor(name, shape, dt))

        def sem(name):
            return ctx.enter_context(nc.semaphore(name))

        resid = sb("resid", [P, TT, D])
        xt_hi = sb("xt_hi", [P, KT, SEQ], F32R)
        xt_lo = sb("xt_lo", [P, KT, SEQ], F32R)
        hid_hi = sb("hid_hi", [P, BT, SEQ], F32R)
        hid_lo = sb("hid_lo", [P, BT, SEQ], F32R)
        w_hi = sb("w_hi", [P, 2, 5 * PIECE], F32R)
        w_lo = sb("w_lo", [P, 2, 5 * PIECE], F32R)
        raw = sb("raw", [P, NRAW, PIECE])
        tmp = sb("tmp", [P, NTMP, HALF])
        gb_rows = sb("gb_rows", [P, 2, D])
        scratch = sb("scratch", [P, 6144])
        shared = sb("shared", [P, 512])
        ident = sb("ident", [P, P])
        ws_t = sb("ws_t", [P, 4, P])
        cols = sb("cols", [P, ROWS])
        inv_cnt = sb("inv_cnt", [P, PAD])
        bn6 = sb("bn6", [P, HT, 6])
        mean_var = sb("mean_var", [P, HT, 2])
        row_sum = sb("row_sum", [P, 2, HT, 2])
        neg_mean = sb("neg_mean", [P, 2, HT])
        squares = sb("squares", [P, 2, HT])
        var_eps = sb("var_eps", [P, 2, HT])
        std = sb("std", [P, 2, HT])
        rstd = sb("rstd", [P, 2, HT])
        newton = sb("newton", [P, 2, HT])
        neg_mean_rstd = sb("neg_mean_rstd", [P, 2, HT])

        v_n = scratch[:, 0:4096].rearrange("p (t c) -> p t c", t=TT)
        u_t = scratch[:, 4096:6144].rearrange("p (g s) -> p g s", g=BT)
        a_t = scratch[:, 0:2 * (PAD + SEQ)].rearrange("p (g s) -> p g s", g=BT)
        win0 = 2 * (PAD + SEQ)
        win = scratch[:, win0:win0 + 2 * (PAD + HALF)].rearrange("p (b s) -> p b s", b=2)
        pooled0 = win0 + 2 * (PAD + HALF)
        pooled = scratch[:, pooled0:pooled0 + 2 * SEQ].rearrange("p (g s) -> p g s", g=BT)
        cv = scratch[:, 0:2 * SEQ].rearrange("p (g s) -> p g s", g=BT)
        z = scratch[:, 2 * SEQ:2 * SEQ + 2 * (SEQ + 2)].rearrange("p (g s) -> p g s", g=BT)
        p_n = scratch[:, 0:TT * PLE].rearrange("p (t k) -> p t k", t=TT)
        ws_n = scratch[:, 4096:4608].rearrange("p (h s) -> p h s", h=4)
        rows_n = scratch[0:ROWS, 4608:4736]
        unread = scratch[:, 5632:6144].bitcast(mybir.dt.bfloat16)
        pool_w = shared[:, :].rearrange("p (g d) -> p g d", g=4)
        sig = shared[:, :].rearrange("p (b c) -> p b c", b=2)
        sgu_b = gb_rows[:, 0, 512:1024].rearrange("p (h t) -> p h t", h=4)

        bank_a = [ctx.enter_context(nc.psum_tensor(f"bank_a{k}", [P, HALF], F32)) for k in range(RING)]
        bank_b = [ctx.enter_context(nc.psum_tensor(f"bank_b{k}", [P, HALF], F32)) for k in range(RING)]

        x_in = [[sem(f"x_in{h}{c}") for c in range(4)] for h in range(2)]
        param_in = sem("param_in")
        late_in = sem("late_in")
        gb_in = sem("gb_in")
        p_in = sem("p_in")
        raw_in = [sem(f"raw_in{k}") for k in range(NRAW)]
        hi_split = sem("hi_split")
        lo_split = sem("lo_split")
        a_full = sem("a_full")
        b_full = sem("b_full")
        b_free = sem("b_free")
        act_value = sem("act_value")
        dve_value = sem("dve_value")
        moved = sem("moved")
        mix_read = sem("mix_read")
        z_ready = sem("z_ready")
        conv_step = sem("conv_step")
        window_step = sem("window_step")
        unit_hi = sem("unit_hi")
        unit_lo = sem("unit_lo")
        var_ready = sem("var_ready")
        std_ready = sem("std_ready")
        norm_ready = sem("norm_ready")
        xn_act = sem("xn_act")
        xn_dve = sem("xn_dve")
        vn_ready = sem("vn_ready")
        mean_ready = sem("mean_ready")
        squared = sem("squared")
        gained = sem("gained")
        gb_scaled = sem("gb_scaled")
        acc_ready = sem("acc_ready")
        sig_ready = sem("sig_ready")
        x_new = sem("x_new")
        ln_step = sem("ln_step")
        ident_step = sem("ident_step")
        dve_const = sem("dve_const")
        out_done = sem("out_done")

        sem_of = dict(aval=act_value, moved=moved, mixg=mix_read, conv=z_ready, dval=dve_value, ga=a_full, gb=b_full,
                      bread=b_free)
        banks = dict(A=bank_a, B=bank_b)

        def walk(visit, loop):
            for st in plan:
                if st.kind != "loop":
                    visit(st)
                    continue
                with loop(0, st.trips) as i:
                    for part in st.body:
                        part.i = i
                        visit(part)

        block = ctx.enter_context(nc.Block())

        @block.sync
        def _(sp):
            def column_slab(w, col0):
                v = w.rearrange("(q k p) n -> q p k n", k=2, p=P)
                return [v[q, :, :, bass.ds(col0, BLK)] for q in range(4)]

            def row_slab(w, row0):
                return [w[bass.ds(row0 + (q // 2) * P, P), (q % 2) * PIECE:(q % 2 + 1) * PIECE] for q in range(4)]

            def sources(what, i):
                kind = what[0]
                if kind == "ev":
                    return column_slab(ev_w_in[0], what[1])
                if kind == "od":
                    return column_slab(od_w_in[0], what[1])
                if kind == "w1":
                    return column_slab(ffn_w1[what[1]], (i + 1 if what[2] == "loop" else what[2]) * BLK)
                if kind == "w2":
                    return row_slab(ffn_w2[what[1]], (i + 1 if what[2] == "loop" else what[2]) * BLK)
                if kind == "ev_out":
                    return row_slab(ev_w_out[0], what[1])
                if kind == "od_out":
                    return row_slab(od_w_out[0], what[1])
                ple = ple_w[what[1]].rearrange("(k p) n -> p k n", p=P)
                return column_slab(ple_gate_w[what[1]], what[2] * BLK) + [ple[:, :, bass.ds(what[2] * BLK, BLK)]]

            def load_slab(what, piece, i=0):
                for q, src in enumerate(sources(what, i)):
                    n = piece + q
                    if n >= NRAW:
                        sp.wait_ge(lo_split, n - NRAW + 1 + i * 8)
                    dst = raw[:, n % NRAW, :]
                    if len(src.shape) == 3:
                        dst = dst.rearrange("p (k n) -> p k n", k=2)
                    sp.dma_start(dst, src).then_inc(raw_in[n % NRAW], 16)

            def load_gb(gain, bias, width):
                sp.dma_start(gb_rows[:, 0, 0:width], gain.partition_broadcast(P)).then_inc(gb_in, 16)
                sp.dma_start(gb_rows[:, 1, 0:width], bias.partition_broadcast(P)).then_inc(gb_in, 16)

            def load_x(h, c):
                cols_c, ts = slice(c * BLK, (c + 1) * BLK), slice(h * HT, (h + 1) * HT)
                sp.dma_start(resid[:, ts, cols_c], x_v[:, ts, cols_c]).then_inc(x_in[h][c], 16)

            for c in range(4):
                load_x(0, c)
                sp.dma_start(raw[:, c, :].rearrange("p (k n) -> p k n", k=2), sources(slabs[0][0], 0)[c])\
                    .then_inc(raw_in[c], 16)
            for c in range(4):
                load_x(1, c)
            load_gb(ev_sgu_ln_g[0], ev_sgu_ln_b[0], WIDTH)
            sp.dma_start(sgu_b, ev_sgu_b[0].partition_broadcast(P)).then_inc(late_in, 16)
            sp.dma_start(pool_w, ev_pool_w[0].rearrange("g c d -> c g d")).then_inc(late_in, 16)

            def stage(st):
                if st.first and st.cur + 1 < n_slabs and not st.step and slabs[st.cur + 1] is not None:
                    load_slab(*slabs[st.cur + 1])
                if st.kind == "a" and st.first and st.blk == 0:
                    sp.wait_ge(unit_lo, st.unit)
                    load_gb(ln1_g[0], ln1_b[0], D)
                if st.kind == "c" and st.first and st.blk == 1:
                    sp.wait_ge(x_new, st.xnew)
                    load_gb(ln1_g[1], ln1_b[1], D)
                if st.kind == "gate" and st.layer == 1 and st.col >= 2:
                    c = slice(0, 3 * BLK) if st.col == 2 else slice(3 * BLK, D)
                    for k, t in enumerate(st.tiles):
                        sp.wait_ge(x_new, st.xnew + k + 1)
                        sp.dma_start(out_v[:, t, c], resid[:, t, c]).then_inc(out_done, 16)

            for st in plan:
                if st.kind != "loop":
                    stage(st)
                    continue
                layer = st.layer
                sp.wait_ge(acc_ready, st.accd)
                load_gb(ln2_g[layer], ln2_b[layer], D)
                sp.wait_ge(unit_lo, st.unit)
                sp.dma_start(p_n, p[layer, 0].rearrange("(t q) k -> q t k", q=P)).then_inc(p_in, 16)
                first = slabs[st.body[0].cur]
                second = slabs[st.body[2].cur]
                with sp.Fori(0, st.trips) as i:
                    load_slab(second[0], second[1], i)
                    for q, src in enumerate(column_slab(ffn_w1[layer], (i + 2) * BLK)):
                        n = first[1] + 8 + q
                        sp.wait_ge(lo_split, n - NRAW + 1 + i * 8)
                        dst = raw[:, n % NRAW, :].rearrange("p (k n) -> p k n", k=2)
                        sp.dma_start(dst, src).then_inc(raw_in[n % NRAW], 16)
            sp.wait_ge(out_done, 2 * 16 * TT)

        @block.gpsimd
        def _(pool):
            pool.memset(ident[:, :], 0.0).then_inc(ident_step, 1)
            pool.wait_ge(ident_step, 1)
            pool.affine_select(out=ident[:, :], in_=ident[:, :], compare_op=ALU.not_equal, fill=1.0, base=0,
                               pattern=[[-1, P]], channel_multiplier=1).then_inc(ident_step, 1)
            def split_low(slab, piece, count, i=0):
                for q in range(count):
                    n = piece + q
                    pool.wait_ge(hi_split, n + 1 + i * 8)
                    s = slice(q * PIECE, (q + 1) * PIECE)
                    pool.tensor_tensor(w_lo[:, slab % 2, s], raw[:, n % NRAW, :], w_hi[:, slab % 2, s].bitcast(F32),
                                       ALU.subtract).then_inc(lo_split, 1)

            split_low(0, 0, 4)
            pool.wait_ge(param_in, 16 * 7)
            pool.affine_select(out=ws_n, in_=ws_n, compare_op=ALU.is_ge, fill=0.0, base=0,
                               pattern=[[0, 4], [-1, P]], channel_multiplier=1).then_inc(ident_step, 1)

            def stage(st):
                if st.split_next and st.cur + 1 < n_slabs:
                    if st.step:
                        split_low(st.cur + 1, st.piece, 4, st.i)
                    else:
                        nxt = slabs[st.cur + 1]
                        split_low(st.cur + 1, st.piece, 5 if nxt and nxt[0][0] == "gate" else 4)
                if st.kind == "alpha":
                    pool.wait_ge(sem_of[st.turned[st.half][0]], st.turned[st.half][1])
                    for k in range(HT):
                        t = st.half * HT + k
                        pool.tensor_scalar(resid[:, t, :], resid[:, t, :], ALPHA, 1.0, ALU.mult, ALU.mult)\
                            .then_inc(acc_ready, 1)
                if st.kind == "stats" and st.half == 0 and st.ln % 2 == 0:
                    pool.wait_ge(gb_in, 32 * (st.ln + 2))
                    pool.tensor_scalar(gb_rows[:, :, :], gb_rows[:, :, :], ALPHA, 1.0, ALU.mult, ALU.mult)\
                        .then_inc(gb_scaled, 1)
                if st.kind == "affine":
                    for k in range(HT):
                        t = st.half * HT + k
                        pool.wait_ge(gained, st.ln // 2 * TT + t + 1)
                        pool.tensor_tensor(resid[:, t, :], resid[:, t, :], gb_rows[:, 1, :], ALU.add)\
                            .then_inc(acc_ready, 1)

            walk(stage, pool.Fori)

        @block.scalar
        def _(act):
            def split_high(slab, piece, count, i=0, end=None, at=0):
                for q in range(at, at + count):
                    n = piece + q - at
                    if end is not None and q == 0:
                        act.wait_ge(sem_of[end[0]], end[1])
                    act.wait_ge(raw_in[n % NRAW], 16 * (n // NRAW + 1) + i * 32)
                    act.copy(w_hi[:, slab % 2, q * PIECE:(q + 1) * PIECE], raw[:, n % NRAW, :]).then_inc(hi_split, 1)

            act.dma_start(rows_n[0:16, :], ln1_g.rearrange("l (j p) -> (l j) p", p=P)).then_inc(param_in, 16)
            act.dma_start(rows_n[16:32, :], ln1_b.rearrange("l (j p) -> (l j) p", p=P)).then_inc(param_in, 16)
            act.dma_start(rows_n[32:48, :], ln2_g.rearrange("l (j p) -> (l j) p", p=P)).then_inc(param_in, 16)
            act.dma_start(rows_n[48:64, :], ln2_b.rearrange("l (j p) -> (l j) p", p=P)).then_inc(param_in, 16)
            act.dma_start(rows_n[64:68, :], ev_pool_scale[0].rearrange("(j p) -> j p", p=P)).then_inc(param_in, 16)
            act.dma_start(rows_n[68:92, :], od_conv_w[0].rearrange("k (j p) -> (k j) p", p=P)).then_inc(param_in, 16)
            act.dma_start(ws_n, ev_sgu_w[0].rearrange("h t s -> t h s")).then_inc(param_in, 16)

            def values(st):
                for k in range(len(st.js) if st.kind == "turn" else 2):
                    if st.unit == 0 and k % 2 == 0:
                        split_high(0, k // 2, 1, at=k // 2)
                    if st.ring == "B":
                        act.wait_ge(b_full, st.n("gb", k + 1))
                        src = bank_b[(st.gb + k) % RING][:, :]
                    else:
                        act.wait_ge(a_full, st.n("ga", k + 1))
                        src = bank_a[(st.ga + k) % RING][:, :]
                    if st.unit + k >= NTMP:
                        act.wait_ge(unit_lo, st.n("unit", k - NTMP + 1))
                    dst = tmp[:, (st.unit + k) % NTMP, :]
                    if st.kind == "ffn":
                        act.activation(dst, src, ACT.Relu).then_inc(act_value, 1)
                    elif st.kind == "lin":
                        g = ROW_POOL + st.blk * BT + k
                        act.activation(dst, src, ACT.Copy, scale=cols[:, g:g + 1]).then_inc(act_value, 1)
                    elif st.kind == "turn" and st.source == "ln":
                        g = ROW_G[st.ln % 2] + st.ln // 2 * KT + st.js[k]
                        b = ROW_B[st.ln % 2] + st.ln // 2 * KT + st.js[k]
                        act.activation(dst, src, ACT.Identity, scale=cols[:, g:g + 1], bias=cols[:, b:b + 1])\
                            .then_inc(act_value, 1)
                    else:
                        act.copy(dst, src).then_inc(act_value, 1)

            def stage(st):
                if st.split_next and st.cur + 1 < n_slabs:
                    end = None
                    if st.cur >= 1:
                        name, value = slab_end[st.cur - 1]
                        end = (name, st.later(value, name))
                    if st.step:
                        split_high(st.cur + 1, st.piece, 4, st.i, end)
                    else:
                        nxt = slabs[st.cur + 1]
                        split_high(st.cur + 1, st.piece, 5 if nxt and nxt[0][0] == "gate" else 4, 0, end)
                if st.kind == "consts":
                    act.wait_ge(a_full, st.ga + 1)
                    act.copy(cols[:, :], bank_a[st.ga % RING][:, 0:ROWS]).then_inc(moved, 1)
                    act.wait_ge(a_full, st.ga + 2)
                    act.copy(ws_t[:, :, :], bank_a[(st.ga + 1) % RING][:, :].rearrange("p (h t) -> p h t", h=4))\
                        .then_inc(moved, 1)
                if st.kind in ("turn", "turn_p", "ffn", "lin") and not st.early:
                    values(st)
                if st.kind in ("u", "a", "c"):
                    if st.half == 0 and (st.kind != "a" or st.g == 0):
                        act.wait_ge(unit_lo, st.unit)
                    for k in ([st.g] if st.kind == "a" else range(BT)):
                        j = 0 if st.kind == "a" else k
                        act.wait_ge(a_full, st.ga + j + 1)
                        s = slice(st.half * HALF, (st.half + 1) * HALF)
                        if st.kind == "a":
                            dst = a_t[:, k, PAD + st.half * HALF:PAD + (st.half + 1) * HALF]
                        else:
                            dst = (u_t if st.kind == "u" else cv)[:, k, s]
                        act.copy(dst, bank_a[(st.ga + j) % RING][:, :]).then_inc(moved, 1)
                if st.sums is not None:
                    for k, t in enumerate(st.tiles):
                        if k == len(st.tiles) - 1:
                            for turn in st.inner:
                                values(turn)
                        act.wait_ge(mean_ready, st.sq + k + 1)
                        if st.sq + k:
                            act.wait_ge(squared, st.sq + k)
                        act.activation(unread, resid[:, t, :], ACT.Square,
                                       bias=neg_mean[:, t // HT, t % HT:t % HT + 1],
                                       accum_out=squares[:, t // HT, t % HT:t % HT + 1]).then_inc(squared, 1)
                if st.kind in ("vln", "stats"):
                    m = st.half if st.kind == "vln" else 2 + 2 * st.ln + st.half
                    act.wait_ge(var_ready, m + 1)
                    act.activation(std[:, st.half, :], var_eps[:, st.half, :], ACT.Sqrt).then_inc(std_ready, 1)
                    if st.kind == "stats":
                        act.wait_ge(norm_ready, 2 * st.ln + st.half + 1)
                        for k in range(2):
                            t = st.half * HT + k
                            act.activation(resid[:, t, :], resid[:, t, :], ACT.Identity,
                                           scale=rstd[:, st.half, k:k + 1],
                                           bias=neg_mean_rstd[:, st.half, k:k + 1]).then_inc(xn_act, 1)
                if st.kind == "gate":
                    for k, t in enumerate(st.tiles):
                        if k == len(st.tiles) - 1:
                            for turn in st.inner if len(st.tiles) == HT else ():
                                values(turn)
                        act.wait_ge(b_full, st.gb + k + 1)
                        if st.xnew + k >= 2:
                            act.wait_ge(x_new, st.xnew + k - 1)
                        else:
                            act.wait_ge(a_full, st.ga)
                        act.activation(sig[:, (st.xnew + k) % 2, :], bank_b[(st.gb + k) % RING][:, 0:BLK],
                                       ACT.Sigmoid).then_inc(sig_ready, 1)

            walk(stage, act.Fori)

        @block.vector
        def _(dve):
            steps = [0]

            def link(ins):
                steps[0] += 1
                ins.then_inc(ln_step, 1)
                dve.wait_ge(ln_step, steps[0])

            for t in range(PAD):
                dve.memset(inv_cnt[:, t:t + 1], 1.0 / (t + 1)).then_inc(dve_const, 1)
            windows = [0]
            convs = [0]

            def target(st, k):
                s = slice(st.half * HALF, (st.half + 1) * HALF)
                if st.kind == "turn":
                    return xt_hi[:, st.js[k], s], xt_lo[:, st.js[k], s]
                return hid_hi[:, k, s], hid_lo[:, k, s]

            def put_high(st, k):
                dve.tensor_copy(target(st, k)[0], tmp[:, (st.unit + k) % NTMP, :]).then_inc(unit_hi, 1)

            def put_low(st, k):
                dve.wait_ge(unit_hi, st.n("unit", k + 1))
                hi, lo = target(st, k)
                dve.tensor_tensor(lo, tmp[:, (st.unit + k) % NTMP, :], hi.bitcast(F32), ALU.subtract)\
                    .then_inc(unit_lo, 1)

            def inverse_root(m, h):
                r, n, v = rstd[:, h, :], newton[:, h, :], var_eps[:, h, :]
                dve.wait_ge(std_ready, m + 1)
                link(dve.reciprocal(r, std[:, h, :]))
                link(dve.tensor_tensor(n, r, r, ALU.mult))
                link(dve.scalar_tensor_tensor(out=n, in0=n, scalar=-0.5, in1=v, op0=ALU.mult, op1=ALU.mult))
                link(dve.scalar_tensor_tensor(out=r, in0=n, scalar=1.5, in1=r, op0=ALU.add, op1=ALU.mult))

            def stage(st):
                if st.kind in ("turn", "turn_p", "lin"):
                    count = len(st.js) if st.kind == "turn" else 2
                    for k in range(count + 1):
                        if k < count:
                            dve.wait_ge(act_value, st.n("aval", k + 1))
                            put_high(st, k)
                        if k >= 1:
                            put_low(st, k - 1)

                if st.kind == "ffn":
                    for k in range(2):
                        dve.wait_ge(act_value, st.n("aval", k + 1))
                        t = tmp[:, (st.unit + k) % NTMP, :]
                        dve.tensor_tensor(t, t, t, ALU.mult).then_inc(dve_value, 1)
                        dve.wait_ge(dve_value, st.n("dval", k + 1))
                        put_high(st, k)
                        put_low(st, k)

                if st.kind == "out":
                    for k in range(2 * len(st.tiles)):
                        t, n = st.tiles[k // 2], k % 2
                        r = resid[:, t, n * HALF:(n + 1) * HALF]
                        if n == 0 and not st.step:
                            dve.wait_ge(acc_ready, st.accd - TT + t + 1)
                        dve.wait_ge(b_full, st.n("gb", k + 1))
                        dve.wait_ge(b_free, st.n("bread", k - 7))
                        src = bank_b[(st.gb + k) % RING][:, :]
                        if st.sums is None:
                            dve.tensor_tensor(r, r, src, ALU.add).then_inc(b_free, 1)
                            continue
                        total = row_sum[:, t // HT, t % HT, :]
                        dve.scalar_tensor_tensor(out=r, in0=r, scalar=1.0, in1=src, op0=ALU.mult, op1=ALU.add,
                                                 accum_out=total[:, n:n + 1]).then_inc(b_free, 1)
                        if n == 1:
                            dve.wait_ge(b_free, st.bread + k + 1)
                            dve.tensor_scalar(neg_mean[:, t // HT, t % HT:t % HT + 1], total[:, 0:1], total[:, 1:2],
                                              -1.0 / D, ALU.add, ALU.mult).then_inc(mean_ready, 1)

                if st.kind == "v":
                    for k, t in enumerate(st.tiles):
                        dve.wait_ge(b_full, st.gb + k + 1)
                        dve.tensor_copy(v_n[:, t, st.col * BLK:(st.col + 1) * BLK],
                                        bank_b[(st.gb + k) % RING][:, 0:BLK]).then_inc(b_free, 1)

                if st.kind == "vln":
                    if st.half == 0:
                        dve.wait_ge(gb_in, 32)
                    dve.wait_ge(b_free, st.bread)
                    for k in range(HT):
                        ins = dve.bn_stats(bn6[:, k, :], v_n[:, st.half * HT + k, :])
                    link(ins)
                    for k in range(HT):
                        ins = dve.bn_aggr(mean_var[:, k, :], bn6[:, k, :])
                    link(ins)
                    dve.tensor_scalar(var_eps[:, st.half, :], mean_var[:, :, 1], EPS, None, ALU.add)\
                        .then_inc(var_ready, 1)
                    inverse_root(st.half, st.half)
                    for k in range(HT):
                        v = v_n[:, st.half * HT + k, :]
                        ins = dve.tensor_scalar(v, v, mean_var[:, k, 0:1], rstd[:, st.half, k:k + 1],
                                                ALU.subtract, ALU.mult)
                    link(ins)
                    for k in range(HT):
                        v = v_n[:, st.half * HT + k, :]
                        ins = dve.tensor_tensor(v, v, gb_rows[:, 0, 0:WIDTH], ALU.mult)
                    link(ins)
                    for k in range(HT):
                        v = v_n[:, st.half * HT + k, :]
                        dve.tensor_tensor(v, v, gb_rows[:, 1, 0:WIDTH], ALU.add).then_inc(vn_ready, 1)

                if st.kind == "stats":
                    m, h = 2 * st.ln + st.half, st.half
                    dve.wait_ge(squared, st.sq)
                    if m >= 2:
                        dve.wait_ge(xn_act, 2 * (m - 1))
                    dve.tensor_scalar(var_eps[:, h, :], squares[:, h, :], 1.0 / D, EPS, ALU.mult, ALU.add)\
                        .then_inc(var_ready, 1)
                    inverse_root(2 + m, h)
                    dve.tensor_tensor(neg_mean_rstd[:, h, :], neg_mean[:, h, :], rstd[:, h, :], ALU.mult)\
                        .then_inc(norm_ready, 1)
                    for k in range(2, HT):
                        r = resid[:, h * HT + k, :]
                        dve.tensor_scalar(r, r, neg_mean[:, h, k:k + 1], rstd[:, h, k:k + 1], ALU.add, ALU.mult)\
                            .then_inc(xn_dve, 1)

                if st.kind == "affine":
                    if st.half == 0:
                        dve.wait_ge(gb_in, 32 * (st.ln + 2))
                        if st.ln % 2 == 0:
                            dve.wait_ge(gb_scaled, st.ln // 2 + 1)
                    dve.wait_ge(sem_of[st.turned[st.half][0]], st.turned[st.half][1])
                    for k in range(HT):
                        r = resid[:, st.half * HT + k, :]
                        dve.tensor_tensor(r, r, gb_rows[:, 0, :], ALU.mult).then_inc(gained, 1)

                if st.kind == "mix":
                    if st.half == 0 and st.blk == 0:
                        dve.wait_ge(late_in, 32)
                    for k in range(2):
                        t = tmp[:, (st.unit + k) % NTMP, :]
                        bias = sgu_b[:, st.blk * BT + k, :].unsqueeze(1).to_broadcast([P, HT, P])
                        dve.wait_ge(a_full, st.ga + k + 1)
                        dve.wait_ge(unit_lo, st.unit + k - NTMP + 1)
                        dve.tensor_tensor(t.rearrange("p (c t) -> p c t", c=HT),
                                          bank_a[(st.ga + k) % RING][:, :].rearrange("p (c t) -> p c t", c=HT),
                                          bias, ALU.add).then_inc(mix_read, 1)
                        dve.wait_ge(mix_read, st.mixg + k + 1)
                        dve.wait_ge(moved, st.moved)
                        dve.tensor_tensor(t, t, u_t[:, k, st.half * HALF:(st.half + 1) * HALF], ALU.mult)\
                            .then_inc(dve_value, 1)
                        dve.wait_ge(dve_value, st.dval + k + 1)
                        put_high(st, k)
                        put_low(st, k)

                if st.kind == "a":
                    g = st.blk * BT + st.g
                    w = WINDOWS[g]
                    k = st.g

                    def wlink(ins):
                        windows[0] += 1
                        ins.then_inc(window_step, 1)
                        dve.wait_ge(window_step, windows[0])

                    if st.half == 0:
                        dve.wait_ge(unit_lo, st.unit)
                        wlink(dve.memset(a_t[:, k, 0:PAD], 0.0))
                    dve.wait_ge(moved, st.moved + 1)
                    src, o, length, history = a_t[:, k, :], PAD + st.half * HALF, 1, w - 2
                    b = 0
                    while length < w:
                        dst = win[:, b, :]
                        n = HALF + history
                        wlink(dve.tensor_tensor(dst[:, PAD - history:PAD + HALF], src[:, o - history:o + HALF],
                                                src[:, o - history - length:o + HALF - length], ALU.add))
                        src, o, b = dst, PAD, 1 - b
                        length *= 2
                        history -= length
                    a = a_t[:, k, PAD + st.half * HALF:PAD + (st.half + 1) * HALF]
                    q = pooled[:, k, st.half * HALF:(st.half + 1) * HALF]
                    wlink(dve.scalar_tensor_tensor(out=q, in0=src[:, PAD:PAD + HALF], scalar=1.0 / w, in1=a,
                                                   op0=ALU.mult, op1=ALU.subtract))
                    if st.half == 0:
                        dve.wait_ge(dve_const, PAD)
                        other = win[:, b, 0:PAD]
                        wlink(dve.scalar_tensor_tensor(out=other, in0=inv_cnt[:, :], scalar=1.0 / w,
                                                       in1=src[:, PAD:2 * PAD], op0=ALU.max, op1=ALU.mult))
                        wlink(dve.tensor_tensor(q[:, 0:PAD], other, a[:, 0:PAD], ALU.subtract))

                if st.kind == "h":
                    def clink(ins):
                        convs[0] += 1
                        ins.then_inc(conv_step, 1)
                        dve.wait_ge(conv_step, convs[0])

                    if st.half == 0 and st.blk == 0:
                        dve.wait_ge(unit_lo, st.unit)
                        clink(dve.memset(z[:, :, 0:2], 0.0))
                    for k in range(2):
                        s = slice(st.half * HALF, (st.half + 1) * HALF)
                        o = 2 + st.half * HALF
                        tile = st.blk * BT + k
                        tap = [cols[:, ROW_CONV + j * KT + tile:ROW_CONV + j * KT + tile + 1] for j in range(3)]
                        dve.wait_ge(a_full, st.ga + k + 1)
                        dve.wait_ge(moved, st.moved)
                        dve.tensor_tensor(z[:, k, o:o + HALF], bank_a[(st.ga + k) % RING][:, :], cv[:, k, s],
                                          ALU.mult).then_inc(z_ready, 1)
                        dve.wait_ge(z_ready, st.conv + k + 1)
                        clink(dve.tensor_scalar(cv[:, k, s], z[:, k, o:o + HALF], tap[2], None, ALU.mult))
                        clink(dve.scalar_tensor_tensor(out=cv[:, k, s], in0=z[:, k, o - 1:o - 1 + HALF],
                                                       scalar=tap[1], in1=cv[:, k, s], op0=ALU.mult, op1=ALU.add))
                        clink(dve.scalar_tensor_tensor(out=cv[:, k, s], in0=z[:, k, o - 2:o - 2 + HALF],
                                                       scalar=tap[0], in1=cv[:, k, s], op0=ALU.mult, op1=ALU.add))

                if st.kind == "bgate":
                    for k in range(2):
                        t = tmp[:, (st.unit + k) % NTMP, :]
                        dve.wait_ge(a_full, st.ga + k + 1)
                        dve.wait_ge(unit_lo, st.unit + k - NTMP + 1)
                        dve.tensor_tensor(t, bank_a[(st.ga + k) % RING][:, :],
                                          cv[:, k, st.half * HALF:(st.half + 1) * HALF], ALU.mult)\
                            .then_inc(dve_value, 1)
                        dve.wait_ge(dve_value, st.dval + k + 1)
                        put_high(st, k)
                        put_low(st, k)

                if st.kind == "gate":
                    if st.first and st.col == 0:
                        dve.wait_ge(gb_in, 32 * (st.layer * 2 + 3))
                    for k, t in enumerate(st.tiles):
                        c = slice(st.col * BLK, (st.col + 1) * BLK)
                        s = sig[:, (st.xnew + k) % 2, :]
                        r = resid[:, t, c]
                        if st.col == 0:
                            half = st.turned[t // HT]
                            dve.wait_ge(sem_of[half[0]], half[1])
                        link(dve.tensor_tensor(r, r, gb_rows[:, 0, c], ALU.mult))
                        dve.tensor_tensor(r, r, gb_rows[:, 1, c], ALU.add).then_inc(ln_step, 1)
                        steps[0] += 1
                        dve.wait_ge(sig_ready, st.xnew + k + 1)
                        dve.tensor_tensor(s, s, bank_b[(st.gb + k) % RING][:, BLK:2 * BLK], ALU.mult)\
                            .then_inc(b_free, 1)
                        dve.wait_ge(ln_step, steps[0])
                        dve.wait_ge(b_free, st.bread + k + 1)
                        dve.tensor_tensor(r, r, s, ALU.add).then_inc(x_new, 1)

            walk(stage, dve.Fori)

        @block.tensor
        def _(pe):
            def free_bank(ring, st, k):
                g = (st.ga if ring == "A" else st.gb) + k
                if g >= RING:
                    name, value = freed[ring][g - RING]
                    pe.wait_ge(sem_of[name], st.later(value, name))
                return banks[ring][g % RING]

            def product(dst, stationary, moving, first, last):
                (s_hi, s_lo), (m_hi, m_lo) = stationary, moving
                pe.matmul(dst, s_hi, m_hi, start=first, stop=False)
                pe.matmul(dst, s_hi, m_lo, start=False, stop=False)
                return pe.matmul(dst, s_lo, m_hi, start=False, stop=last)

            def xt(j, s):
                return xt_hi[:, j, s], xt_lo[:, j, s]

            def hid(j, s):
                return hid_hi[:, j, s], hid_lo[:, j, s]

            def slot(st, at, count):
                s = st.cur % 2
                return w_hi[:, s, at:at + count], w_lo[:, s, at:at + count]

            def turn_groups(st, ks):
                if st.source == "input" and 0 in ks:
                    pe.wait_ge(ident_step, 2)
                if 0 in ks:
                    if st.kind == "turn_p":
                        pe.wait_ge(p_in, 16 * (st.layer + 1))
                    elif st.source == "ln":
                        pe.wait_ge(xn_act, 2 * (2 * st.ln + st.half + 1))
                        pe.wait_ge(xn_dve, 2 * (2 * st.ln + st.half + 1))
                    elif st.source == "gate":
                        pe.wait_ge(x_new, 3 * TT + (st.half + 1) * HT)
                for k in ks:
                    if st.source == "input" and st.js[k] % 2 == 0:
                        pe.wait_ge(x_in[st.half][st.js[k] // 2], 16)
                    dst = free_bank(st.ring, st, k)
                    src, j = (p_n, k) if st.kind == "turn_p" else (resid, st.js[k])
                    for t in range(HT):
                        ins = pe.transpose(dst[:, t * P:(t + 1) * P],
                                           src[:, st.half * HT + t, j * P:(j + 1) * P], ident[:, :])
                    ins.then_inc(a_full if st.ring == "A" else b_full, 1)

            def stage(st):
                if st.first and st.cur > 0:
                    pe.wait_ge(lo_split, st.n("piece"))
                if st.kind == "consts":
                    pe.wait_ge(ident_step, 3)
                    pe.wait_ge(param_in, 16 * 7)
                    pe.transpose(free_bank("A", st, 0)[:, 0:ROWS], rows_n, ident[0:ROWS, 0:ROWS]).then_inc(a_full, 1)
                    bank = free_bank("A", st, 1)
                    for h in range(4):
                        ins = pe.transpose(bank[:, h * P:(h + 1) * P], ws_n[:, h, :], ident[:, :])
                    ins.then_inc(a_full, 1)
                if st.kind in ("turn", "turn_p") and not st.nested:
                    turn_groups(st, range(len(st.js) if st.kind == "turn" else 2))
                if st.kind in ("ffn", "u", "a", "c", "h", "bgate"):
                    ks = [st.g] if st.kind == "a" else list(range(BT))
                    cols_of = [slice(k * P, (k + 1) * P) for k in ks]
                    dsts = [None] * len(ks)
                    s = slice(st.half * HALF, (st.half + 1) * HALF)
                    if not st.paced:
                        pe.wait_ge(unit_lo, st.need_x[st.half])
                        for j, k in enumerate(ks):
                            dst = free_bank("A", st, j)[:, :]
                            for q in range(KT):
                                ins = product(dst, slot(st, q * BLK + k * P, P), xt(q, s), q == 0, q == KT - 1)
                            ins.then_inc(a_full, 1)
                    else:
                        dsts = [free_bank("A", st, j)[:, :] for j in range(len(ks))]
                        for q in range(KT):
                            pe.wait_ge(unit_lo, st.need_x[st.half] - KT + q + 1)
                            for j, k in enumerate(ks):
                                ins = product(dsts[j], slot(st, q * BLK + k * P, P), xt(q, s), q == 0, q == KT - 1)
                                if q == KT - 1:
                                    ins.then_inc(a_full, 1)
                            for turn in st.inner:
                                turn_groups(turn, {5: range(0, 2), 6: range(2, 5), 7: range(5, 8)}.get(q, ()))
                if st.kind == "out":
                    for k in range(2 * len(st.tiles)):
                        t, n = st.tiles[k // 2], k % 2
                        if k == 0 or t == HT:
                            pe.wait_ge(unit_lo, st.later(st.need_h[t // HT], "unit"))
                        if k == 2 * len(st.tiles) - 2:
                            for turn in st.inner:
                                turn_groups(turn, range(len(turn.js)))
                        dst = free_bank("B", st, k)[:, :]
                        for q in range(BT):
                            ins = product(dst, hid(q, slice(t * P, (t + 1) * P)), slot(st, q * D + n * HALF, HALF),
                                          q == 0, q == BT - 1)
                        ins.then_inc(b_full, 1)
                if st.kind in ("v", "gate"):
                    h = st.tiles[0] // HT
                    last = KT - 1
                    if not st.paced:
                        pe.wait_ge(unit_lo, st.need_x[h])
                    width = 2 if len(st.tiles) == 2 else 1
                    for k0 in range(0, len(st.tiles), width):
                        ks = range(k0, k0 + width)
                        if width == 1 and k0 == len(st.tiles) - 1:
                            for turn in st.inner:
                                turn_groups(turn, range(len(turn.js)))
                        dsts = [free_bank("B", st, k) for k in ks]
                        for q in range(KT):
                            if st.paced:
                                pe.wait_ge(unit_lo, st.need_x[h] - KT + q + 1)
                            if st.first and st.cur == 0 and k0 == 0:
                                pe.wait_ge(lo_split, q // 2 + 1)
                            for dst, k in zip(dsts, ks):
                                s = slice(st.tiles[k] * P, (st.tiles[k] + 1) * P)
                                ins = product(dst[:, 0:BLK], xt(q, s), slot(st, q * BLK, BLK), q == 0, q == last)
                                if st.kind == "v" and q == last:
                                    ins.then_inc(b_full, 1)
                            for turn in st.inner if width == 2 else ():
                                at = {2: range(0, 4), 4: range(4, 6), 6: range(6, 8)} if turn.kind == "turn" \
                                    else {7: range(0, 2)}
                                turn_groups(turn, at.get(q, ()) if k0 == 0 else ())
                        if st.kind == "gate":
                            pe.wait_ge(unit_lo, st.need_h[h])
                            for dst, k in zip(dsts, ks):
                                s = slice(st.tiles[k] * P, (st.tiles[k] + 1) * P)
                                for q in range(PLE // P):
                                    ins = product(dst[:, BLK:2 * BLK], hid(q, s),
                                                  slot(st, KT * BLK + q * BLK, BLK), q == 0, q == PLE // P - 1)
                                ins.then_inc(b_full, 1)
                if st.kind == "mix":
                    pe.wait_ge(vn_ready, HT * (st.half + 1))
                    pe.wait_ge(moved, 2)
                    for k in range(2):
                        head = st.blk * BT + k
                        dst = free_bank("A", st, k)
                        for c in range(HT):
                            ins = pe.matmul(dst[:, c * P:(c + 1) * P],
                                            v_n[:, st.half * HT + c, head * P:(head + 1) * P], ws_t[:, head, :],
                                            start=True, stop=True)
                        ins.then_inc(a_full, 1)
                if st.kind == "lin":
                    pe.wait_ge(window_step, window_steps(st))
                    pe.wait_ge(late_in, 32)
                    for k in range(2):
                        pe.matmul(free_bank("A", st, k)[:, :], pool_w[:, st.blk * BT + k, :],
                                  pooled[:, k, st.half * HALF:(st.half + 1) * HALF], start=True, stop=True)\
                            .then_inc(a_full, 1)

            def window_steps(st):
                def steps_of(half, g):
                    levels = WINDOWS[g].bit_length() - 1
                    return levels + (4 if half == 0 else 1)
                order = [(b, h, g) for b in range(2) for h in range(2) for g in range(BT)]
                upto = order.index((st.blk, st.half, BT - 1))
                return sum(steps_of(h, b * BT + g) for b, h, g in order[:upto + 1])

            walk(stage, pe.Fori)


_INS = ["x", "p", "ev_w_in", "ev_pool_w", "ev_pool_scale", "ev_sgu_ln_g", "ev_sgu_ln_b", "ev_sgu_w", "ev_sgu_b",
        "ev_w_out", "od_w_in", "od_conv_w", "od_w_out", "ln1_g", "ln1_b", "ffn_w1", "ffn_w2", "ln2_g", "ln2_b",
        "ple_gate_w", "ple_w"]


def kernel(**inputs):
    import numpy as _np
    import concourse.bacc as _bacc
    from concourse import mybir as _mybir
    from concourse.bass_utils import run_bass_kernel_spmd as _run

    nc = _bacc.Bacc("TRN2", target_bir_lowering=False, num_devices=1)
    arrays, args = {}, []
    for name in _INS:
        a = _np.ascontiguousarray(inputs[name])
        arrays[f"in_{name}_dram"] = a
        args.append(nc.dram_tensor(f"in_{name}_dram", a.shape, _mybir.dt.from_np(a.dtype), kind="ExternalInput").ap())
    args.append(nc.dram_tensor("out_dram", (1, SEQ, D), F32, kind="ExternalOutput").ap())
    trunk(nc, *args)
    r = _run(nc, [arrays], core_ids=[0])
    return r.results[0]["out_dram"]
```
